# Optimizing a Trainium2 kernel written in Bass

```python
import math
import jax, jax.numpy as jnp
from jax import lax
import numpy as np
import jax
import jax.numpy as jnp

D_MODEL = 1024
BATCH = 1
SEQ = 256
DEPTH = 2

D_SSM = D_MODEL // 2
SSM_GROUP = 16
SSM_GROUPS = D_SSM // SSM_GROUP
SSM_STATE = 64
DT_MIN = 1e-3
DT_MAX = 1e-1
D_ATTN = D_MODEL - D_SSM
HEAD_DIM = 64
N_HEADS = D_ATTN // HEAD_DIM
MOBA_BLOCK = 256
MOBA_TOPK = 3
Q_CHUNK = 32
REL_BUCKETS = 32
REL_MAX_DIST = 128
CONV_WIDTH = 31
D_CONV = D_MODEL
FFN_HIDDEN = 2816
FFN_CONV_WIDTH = 3
N_EVEN = (DEPTH + 1) // 2
N_ODD = DEPTH // 2
EPS = 1e-6


def rms_norm(x, g):
    xf = x.astype(jnp.float32)
    y = xf * lax.rsqrt(jnp.mean(xf * xf, axis=-1, keepdims=True) + EPS)
    return (y * g.astype(jnp.float32)).astype(x.dtype)

def layer_norm(x, g, b):
    xf = x.astype(jnp.float32)
    mu = jnp.mean(xf, axis=-1, keepdims=True)
    xc = xf - mu
    y = xc * lax.rsqrt(jnp.mean(xc * xc, axis=-1, keepdims=True) + EPS)
    return (y * g.astype(jnp.float32) + b.astype(jnp.float32)).astype(x.dtype)

def causal_dwconv(x, w, b):
    k = w.shape[0]
    xp = jnp.pad(x, ((0, 0), (k - 1, 0), (0, 0)))
    y = lax.conv_general_dilated(xp, w[:, None, :], (1,), 'VALID',
                                 dimension_numbers=('NWC', 'WIO', 'NWC'),
                                 feature_group_count=x.shape[-1])
    return y + b

def modulate(h, shift, scale):
    return h * (1.0 + scale[:, None, :]) + shift[:, None, :]

def s5_mixer(u, a_re, a_im, log_dt, b_re, b_im, c_re, c_im, d_skip, glu_w, glu_b):
    bsz, seq_len, _ = u.shape
    f32 = jnp.float32
    uf = u.astype(f32).reshape(bsz, seq_len, SSM_GROUPS, SSM_GROUP)
    lam_re = a_re.astype(f32)
    lam_im = a_im.astype(f32)
    dt = jnp.exp(log_dt.astype(f32))[:, None]
    mag = jnp.exp(lam_re * dt)
    ab_re = mag * jnp.cos(lam_im * dt)
    ab_im = mag * jnp.sin(lam_im * dt)
    den = lam_re * lam_re + lam_im * lam_im
    nr = ab_re - 1.0
    coef_re = (nr * lam_re + ab_im * lam_im) / den
    coef_im = (ab_im * lam_re - nr * lam_im) / den
    br = b_re.astype(f32)
    bi = b_im.astype(f32)
    bb_re = coef_re[..., None] * br - coef_im[..., None] * bi
    bb_im = coef_re[..., None] * bi + coef_im[..., None] * br
    bu_re = jnp.einsum('blgh,gph->blgp', uf, bb_re)
    bu_im = jnp.einsum('blgh,gph->blgp', uf, bb_im)
    a_full_re = jnp.broadcast_to(ab_re, (1, seq_len) + ab_re.shape)
    a_full_im = jnp.broadcast_to(ab_im, (1, seq_len) + ab_im.shape)

    def combine(e1, e2):
        a1r, a1i, b1r, b1i = e1
        a2r, a2i, b2r, b2i = e2
        return (a1r * a2r - a1i * a2i,
                a1r * a2i + a1i * a2r,
                a2r * b1r - a2i * b1i + b2r,
                a2r * b1i + a2i * b1r + b2i)

    _, _, xr, xi = lax.associative_scan(combine, (a_full_re, a_full_im, bu_re, bu_im), axis=1)
    y = (jnp.einsum('blgp,ghp->blgh', xr, c_re.astype(f32))
         - jnp.einsum('blgp,ghp->blgh', xi, c_im.astype(f32))
         + d_skip.astype(f32) * uf)
    y = jax.nn.gelu(y.reshape(bsz, seq_len, D_SSM)).astype(u.dtype)
    return y * jax.nn.sigmoid(y @ glu_w + glu_b)

def rel_bucket(dist):
    n = jnp.maximum(dist, 0)
    max_exact = REL_BUCKETS // 2
    nf = jnp.maximum(n, 1).astype(jnp.float32)
    large = max_exact + (jnp.log(nf / max_exact) / math.log(REL_MAX_DIST / max_exact)
                         * (REL_BUCKETS - max_exact)).astype(jnp.int32)
    large = jnp.minimum(large, REL_BUCKETS - 1)
    return jnp.where(n < max_exact, n, large)

def moba_attention(q, k, v, rel_bias):
    bsz, seq_len = q.shape[:2]
    f32 = jnp.float32
    n_blocks = -(-seq_len // MOBA_BLOCK)
    l_pad = n_blocks * MOBA_BLOCK
    pad = ((0, 0), (0, l_pad - seq_len), (0, 0), (0, 0))
    q, k, v = [jnp.pad(t, pad).transpose(0, 2, 1, 3) for t in (q, k, v)]
    kb = k.reshape(bsz, N_HEADS, n_blocks, MOBA_BLOCK, HEAD_DIM)
    vb = v.reshape(bsz, N_HEADS, n_blocks, MOBA_BLOCK, HEAD_DIM)
    k_mean = jnp.mean(kb.astype(f32), axis=3).astype(q.dtype)
    top = min(MOBA_TOPK, n_blocks)
    scale = HEAD_DIM ** -0.5
    bias_tab = rel_bias.astype(f32)
    b_idx = jnp.arange(bsz)[:, None, None, None]
    h_idx = jnp.arange(N_HEADS)[None, :, None, None]
    h_bias = jnp.arange(N_HEADS)[None, :, None, None, None]
    offs = jnp.arange(MOBA_BLOCK)

    def chunk(ci):
        start = ci * Q_CHUNK
        blk = start // MOBA_BLOCK
        q_c = lax.dynamic_slice_in_dim(q, start, Q_CHUNK, axis=2)
        q_pos = start + jnp.arange(Q_CHUNK)
        gate = jnp.einsum('bhqd,bhnd->bhqn', q_c, k_mean).astype(f32)
        gate = jnp.where(jnp.arange(n_blocks) < blk, gate, -jnp.inf)
        _, sel = lax.top_k(gate, top)
        sel_valid = jnp.arange(top) < blk
        k_sel = kb[b_idx, h_idx, sel]
        v_sel = vb[b_idx, h_idx, sel]
        k_own = lax.dynamic_index_in_dim(kb, blk, axis=2, keepdims=False)
        v_own = lax.dynamic_index_in_dim(vb, blk, axis=2, keepdims=False)
        s_sel = jnp.einsum('bhqd,bhqrtd->bhqrt', q_c, k_sel).astype(f32) * scale
        k_pos_sel = sel[..., None] * MOBA_BLOCK + offs
        s_sel = s_sel + bias_tab[rel_bucket(q_pos[:, None, None] - k_pos_sel), h_bias]
        s_sel = jnp.where(sel_valid[:, None], s_sel, -jnp.inf)
        dist_own = q_pos[:, None] - (blk * MOBA_BLOCK + offs)[None, :]
        s_own = jnp.einsum('bhqd,bhtd->bhqt', q_c, k_own).astype(f32) * scale
        s_own = s_own + bias_tab[rel_bucket(dist_own)].transpose(2, 0, 1)
        s_own = jnp.where(dist_own >= 0, s_own, -jnp.inf)
        scores = jnp.concatenate(
            [s_sel.reshape(bsz, N_HEADS, Q_CHUNK, top * MOBA_BLOCK), s_own], axis=-1)
        p = jax.nn.softmax(scores, axis=-1).astype(v.dtype)
        p_sel = p[..., :top * MOBA_BLOCK].reshape(bsz, N_HEADS, Q_CHUNK, top, MOBA_BLOCK)
        p_own = p[..., top * MOBA_BLOCK:]
        return (jnp.einsum('bhqrt,bhqrtd->bhqd', p_sel, v_sel)
                + jnp.einsum('bhqt,bhtd->bhqd', p_own, v_own))

    out = lax.map(chunk, jnp.arange(l_pad // Q_CHUNK))
    out = out.transpose(1, 0, 3, 2, 4).reshape(bsz, l_pad, N_HEADS * HEAD_DIM)
    return out[:, :seq_len]

def conformer_conv(h, w_in, b_in, dw_w, dw_b, ln_g, ln_b, w_out, b_out):
    a = h @ w_in + b_in
    a = a[..., :D_CONV] * jax.nn.sigmoid(a[..., D_CONV:])
    a = causal_dwconv(a, dw_w, dw_b)
    a = jax.nn.silu(layer_norm(a, ln_g, ln_b))
    return a @ w_out + b_out

def conv_ffn(h, w_up, w_gate, dw_w, dw_b, w_down):
    g = causal_dwconv(h @ w_gate, dw_w, dw_b)
    return (jax.nn.silu(g) * (h @ w_up)) @ w_down

def first_inputs(seed: int = 0) -> dict:
    key = jax.random.key(seed)
    ks = iter(jax.random.split(key, 40))

    def nrm(shape, scale):
        return scale * jax.random.normal(next(ks), shape, jnp.float32)

    G, H, P = SSM_GROUPS, SSM_GROUP, SSM_STATE
    n_idx = jnp.arange(P, dtype=jnp.float32)
    return {
        'x': nrm((BATCH, SEQ, D_MODEL), 1.0),
        'c': nrm((BATCH, D_MODEL), 1.0),
        'mod_w': nrm((DEPTH, D_MODEL, 6 * D_MODEL), 0.5 * D_MODEL ** -0.5),
        'mod_b': nrm((DEPTH, 6 * D_MODEL), 0.01),
        'norm_g': 1.0 + nrm((DEPTH, 2, D_MODEL), 0.01),
        'final_g': 1.0 + nrm((D_MODEL,), 0.01),
        'ab_w_in': nrm((N_EVEN, D_MODEL, D_SSM + 3 * D_ATTN), D_MODEL ** -0.5),
        'ssm_a_re': -0.5 + nrm((N_EVEN, G, P), 0.01),
        'ssm_a_im': math.pi * n_idx + nrm((N_EVEN, G, P), 0.01),
        'ssm_log_dt': jax.random.uniform(next(ks), (N_EVEN, G), jnp.float32,
                                         math.log(DT_MIN), math.log(DT_MAX)),
        'ssm_b_re': nrm((N_EVEN, G, P, H), (2 * H) ** -0.5),
        'ssm_b_im': nrm((N_EVEN, G, P, H), (2 * H) ** -0.5),
        'ssm_c_re': nrm((N_EVEN, G, H, P), P ** -0.5),
        'ssm_c_im': nrm((N_EVEN, G, H, P), P ** -0.5),
        'ssm_d': nrm((N_EVEN, G, H), 1.0),
        'ssm_glu_w': nrm((N_EVEN, D_SSM, D_SSM), D_SSM ** -0.5),
        'ssm_glu_b': nrm((N_EVEN, D_SSM), 0.01),
        'ab_w_out': nrm((N_EVEN, D_MODEL, D_MODEL), D_MODEL ** -0.5),
        'rel_bias': nrm((REL_BUCKETS, N_HEADS), 0.5),
        'cm_w_in': nrm((N_ODD, D_MODEL, 2 * D_CONV), D_MODEL ** -0.5),
        'cm_b_in': nrm((N_ODD, 2 * D_CONV), 0.01),
        'cm_dw_w': nrm((N_ODD, CONV_WIDTH, D_CONV), CONV_WIDTH ** -0.5),
        'cm_dw_b': nrm((N_ODD, D_CONV), 0.01),
        'cm_ln_g': 1.0 + nrm((N_ODD, D_CONV), 0.01),
        'cm_ln_b': nrm((N_ODD, D_CONV), 0.01),
        'cm_w_out': nrm((N_ODD, D_CONV, D_MODEL), D_CONV ** -0.5),
        'cm_b_out': nrm((N_ODD, D_MODEL), 0.01),
        'ffn_w_up': nrm((DEPTH, D_MODEL, FFN_HIDDEN), D_MODEL ** -0.5),
        'ffn_w_gate': nrm((DEPTH, D_MODEL, FFN_HIDDEN), D_MODEL ** -0.5),
        'ffn_dw_w': nrm((DEPTH, FFN_CONV_WIDTH, FFN_HIDDEN), FFN_CONV_WIDTH ** -0.5),
        'ffn_dw_b': nrm((DEPTH, FFN_HIDDEN), 0.01),
        'ffn_w_down': nrm((DEPTH, FFN_HIDDEN, D_MODEL), FFN_HIDDEN ** -0.5),
    }

def first_block(x, c, mod_w, mod_b, norm_g, final_g, ab_w_in, ssm_a_re, ssm_a_im, ssm_log_dt,
              ssm_b_re, ssm_b_im, ssm_c_re, ssm_c_im, ssm_d, ssm_glu_w, ssm_glu_b, ab_w_out,
              rel_bias, cm_w_in, cm_b_in, cm_dw_w, cm_dw_b, cm_ln_g, cm_ln_b, cm_w_out, cm_b_out,
              ffn_w_up, ffn_w_gate, ffn_dw_w, ffn_dw_b, ffn_w_down):
    bsz, seq_len, _ = x.shape
    cs = jax.nn.silu(c)
    for layer in range(DEPTH):
        mod = cs @ mod_w[layer] + mod_b[layer]
        sh1, sc1, g1, sh2, sc2, g2 = jnp.split(mod, 6, axis=-1)
        h = modulate(rms_norm(x, norm_g[layer, 0]), sh1, sc1)
        i = layer // 2
        if layer % 2 == 0:
            proj = h @ ab_w_in[i]
            u = proj[..., :D_SSM]
            qkv = proj[..., D_SSM:].reshape(bsz, seq_len, 3, N_HEADS, HEAD_DIM)
            y_ssm = s5_mixer(u, ssm_a_re[i], ssm_a_im[i], ssm_log_dt[i], ssm_b_re[i],
                             ssm_b_im[i], ssm_c_re[i], ssm_c_im[i], ssm_d[i],
                             ssm_glu_w[i], ssm_glu_b[i])
            y_att = moba_attention(qkv[:, :, 0], qkv[:, :, 1], qkv[:, :, 2], rel_bias)
            y = jnp.concatenate([y_ssm, y_att], axis=-1) @ ab_w_out[i]
        else:
            y = conformer_conv(h, cm_w_in[i], cm_b_in[i], cm_dw_w[i], cm_dw_b[i],
                               cm_ln_g[i], cm_ln_b[i], cm_w_out[i], cm_b_out[i])
        x = x + g1[:, None, :] * y
        h = modulate(rms_norm(x, norm_g[layer, 1]), sh2, sc2)
        x = x + g2[:, None, :] * conv_ffn(h, ffn_w_up[layer], ffn_w_gate[layer],
                                          ffn_dw_w[layer], ffn_dw_b[layer], ffn_w_down[layer])
    return rms_norm(x, final_g)


_first_inputs = first_inputs


def first_inputs(seed=0):
    import zlib

    import numpy as np

    out = dict(_first_inputs(seed))
    spreads = {}
    factors = {'mod_b': 3.93,
     'norm_g': 8.0,
     'final_g': 29.97,
     'ssm_a_re': 64.0,
     'ssm_a_im': 58.616,
     'ssm_log_dt': 64.0,
     'ssm_b_re': 64.0,
     'ssm_b_im': 64.0,
     'ssm_c_re': 64.0,
     'ssm_c_im': 64.0,
     'ssm_glu_b': 55.422,
     'rel_bias': 2.818,
     'cm_b_in': 64.0,
     'cm_dw_b': 64.0,
     'cm_ln_g': 64.0,
     'cm_ln_b': 64.0,
     'cm_b_out': 64.0,
     'ffn_dw_b': 31.459}
    for name, (base, spread) in spreads.items():
        noise = np.random.default_rng([zlib.crc32(name.encode()), seed]).standard_normal(out[name].shape)
        drawn = base * np.exp(spread * noise) if base else spread * noise
        out[name] = __import__('jax').numpy.asarray(drawn.astype(out[name].dtype))
    for name, factor in factors.items():
        out[name] = (out[name] * factor).astype(out[name].dtype)
    return out


_narrow_inputs = first_inputs


def first_inputs(seed=0):
    out = dict(_narrow_inputs(seed))
    wider = {'final_g': 6.16, 'cm_ln_g': 8.12, 'cm_ln_b': 7.87, 'cm_b_out': 5.36}
    for name, times in wider.items():
        mean = out[name].mean()
        out[name] = (mean + times * (out[name] - mean)).astype(out[name].dtype)
    return out


GRID_W = 64
CTX_LEN = 256
N_MIXERS = 2
N_MLA = (DEPTH + 1) // 2
N_HYENA = DEPTH // 2

MLA_HEADS = 16
QK_NOPE = 64
QK_ROPE = 32
QK_DIM = QK_NOPE + QK_ROPE
V_HEAD = 64
Q_LORA = 512
KV_LORA = 256
ROPE_THETA = 10000.0
Q_BLOCK = 128

HY_BANDS = 16
HY_POS_DIM = 1 + 2 * HY_BANDS
HY_FILTER_HIDDEN = 64
HY_DECAY_SLOW = math.log(100.0) / 1.5
HY_DECAY_FAST = math.log(100.0) / 0.3
HY_FILTER_INIT = 0.02

D_FF = 2816

F32 = jnp.float32


def rmsnorm(x, g):
    xf = x.astype(F32)
    y = xf * lax.rsqrt(jnp.mean(xf * xf, axis=-1, keepdims=True) + EPS)
    return (y * g.astype(F32)).astype(x.dtype)

def modulate_2(h, shift, scale):
    return h * (1 + scale) + shift

def dwconv3(x, w, b):
    xp = jnp.pad(x, ((0, 0), (1, 1), (0, 0)))
    return xp[:, :-2] * w[0] + xp[:, 1:-1] * w[1] + xp[:, 2:] * w[2] + b

def axial_rope_tables(rows):
    row = jnp.repeat(jnp.arange(rows, dtype=F32), GRID_W)
    col = jnp.tile(jnp.arange(GRID_W, dtype=F32), rows)
    half = QK_ROPE // 2
    inv_freq = ROPE_THETA ** (-jnp.arange(0, half, 2, dtype=F32) / half)
    ang_r = row[:, None] * inv_freq
    ang_c = col[:, None] * inv_freq
    ang = jnp.concatenate([ang_r, ang_r, ang_c, ang_c], axis=-1)
    return jnp.cos(ang), jnp.sin(ang)

def apply_axial_rope(x, cos, sin):
    q = QK_ROPE // 4
    xf = x.astype(F32)
    rot = jnp.concatenate([-xf[..., q:2 * q], xf[..., :q], -xf[..., 3 * q:], xf[..., 2 * q:3 * q]], axis=-1)
    return (xf * cos + rot * sin).astype(x.dtype)

def mla_queries(h, w_dq, g_q, w_uq, cos, sin):
    B, L, _ = h.shape
    cq = rmsnorm(h @ w_dq, g_q)
    q = (cq @ w_uq).reshape(B, L, MLA_HEADS, QK_DIM)
    q_nope, q_pe = q[..., :QK_NOPE], q[..., QK_NOPE:]
    if cos is not None:
        q_pe = apply_axial_rope(q_pe, cos[None, :, None, :], sin[None, :, None, :])
    return jnp.concatenate([q_nope, q_pe], axis=-1)

def mla_keys_values(h, w_dkv, g_kv, w_uk, w_uv, cos, sin):
    B, L, _ = h.shape
    kv = h @ w_dkv
    ckv = rmsnorm(kv[..., :KV_LORA], g_kv)
    k_pe = kv[..., KV_LORA:]
    if cos is not None:
        k_pe = apply_axial_rope(k_pe, cos[None], sin[None])
    k_nope = (ckv @ w_uk).reshape(B, L, MLA_HEADS, QK_NOPE)
    v = (ckv @ w_uv).reshape(B, L, MLA_HEADS, V_HEAD)
    k_pe = jnp.broadcast_to(k_pe[:, :, None, :], (B, L, MLA_HEADS, QK_ROPE))
    return jnp.concatenate([k_nope, k_pe], axis=-1), v

def block_attention(q, k, v):
    B, Lq, H, dk = q.shape
    nblk = Lq // Q_BLOCK
    scale = 1.0 / math.sqrt(dk)
    qb = q.reshape(B, nblk, Q_BLOCK, H, dk).transpose(1, 0, 2, 3, 4)

    def one_block(qblk):
        s = jnp.einsum('bqhd,bkhd->bhqk', qblk, k).astype(F32) * scale
        p = jax.nn.softmax(s, axis=-1).astype(v.dtype)
        return jnp.einsum('bhqk,bkhd->bqhd', p, v)

    o = lax.map(one_block, qb)
    return o.transpose(1, 0, 2, 3, 4).reshape(B, Lq, H * v.shape[-1])

def hyena_pos_features(L):
    t = jnp.linspace(0.0, 1.0, L, dtype=F32)
    w = 2.0 * math.pi * jnp.arange(L, dtype=F32) / L
    f = jnp.linspace(1e-4, HY_BANDS - 1, HY_BANDS, dtype=F32)
    z = jnp.concatenate([t[:, None], jnp.cos(w[:, None] * f), -jnp.sin(w[:, None] * f)], axis=-1)
    return t, z

def hyena_filters(L, f_w1, f_b1, f_freq1, f_w2, f_b2, f_freq2, f_w3, decay):
    t, z = hyena_pos_features(L)
    h = jnp.sin(f_freq1.astype(F32) * (z @ f_w1.astype(F32) + f_b1.astype(F32)))
    h = jnp.sin(f_freq2.astype(F32) * (h @ f_w2.astype(F32) + f_b2.astype(F32)))
    h = h @ f_w3.astype(F32)
    window = jnp.exp(-t[:, None] * jnp.abs(decay.astype(F32))[None, :])
    d = h.shape[1] // 2
    return h[:, :d] * window, h[:, d:] * window

def two_sided_fftconv(u, h_fwd, h_bwd):
    L = u.shape[1]
    filt = jnp.concatenate([h_fwd, jnp.zeros((1, h_fwd.shape[1]), F32), h_bwd[1:][::-1]], axis=0)
    filt_f = jnp.fft.rfft(filt, n=2 * L, axis=0)
    u_f = jnp.fft.rfft(u.astype(F32), n=2 * L, axis=1)
    y = jnp.fft.irfft(u_f * filt_f[None], n=2 * L, axis=1)[:, :L]
    return y.astype(u.dtype)

def hyena_mixer(u, w_in, b_in, conv_w, conv_b, f_w1, f_b1, f_freq1, f_w2, f_b2, f_freq2, f_w3, decay, d_bias, w_out, b_out):
    L = u.shape[1]
    z = dwconv3(u @ w_in + b_in, conv_w, conv_b)
    x1, x2, v = jnp.split(z, 3, axis=-1)
    h_fwd, h_bwd = hyena_filters(L, f_w1, f_b1, f_freq1, f_w2, f_b2, f_freq2, f_w3, decay)
    v = v * x2
    y = (two_sided_fftconv(v, h_fwd, h_bwd) + v * d_bias) * x1
    return y @ w_out + b_out

def conv_ffn_2(h, w_up, conv_w, conv_b, w_down):
    z = dwconv3(h @ w_up, conv_w, conv_b)
    a, g = jnp.split(z, 2, axis=-1)
    return (jax.nn.silu(g) * a) @ w_down

def second_inputs(seed: int = 0) -> dict:
    key = jax.random.key(seed)
    ks = jax.random.split(key, 40)
    D = D_MODEL

    def nrm(i, shape, scale):
        return jax.random.normal(ks[i], shape, F32) * scale

    def gain(i, shape):
        return 1.0 + nrm(i, shape, 0.05)

    decay_base = jnp.linspace(HY_DECAY_SLOW, HY_DECAY_FAST, D, dtype=F32)
    return {
        'x': nrm(0, (BATCH, SEQ, D), 1.0),
        'c': nrm(1, (BATCH, D), 1.0),
        'ctx': nrm(2, (BATCH, CTX_LEN, D), 1.0),
        'c_ctx': nrm(3, (D,), 1.0),
        'mod_w': nrm(4, (DEPTH, D, 6 * D), D ** -0.5),
        'mod_b': nrm(5, (DEPTH, 6 * D), 0.02),
        'norm_mix_g': gain(6, (DEPTH, D)),
        'norm_ffn_g': gain(7, (DEPTH, D)),
        'mla_w_dq': nrm(8, (N_MLA, D, Q_LORA), D ** -0.5),
        'mla_g_q': gain(9, (N_MLA, Q_LORA)),
        'mla_w_uq': nrm(10, (N_MLA, Q_LORA, MLA_HEADS * QK_DIM), Q_LORA ** -0.5),
        'mla_w_dkv': nrm(11, (N_MLA, D, KV_LORA + QK_ROPE), D ** -0.5),
        'mla_g_kv': gain(12, (N_MLA, KV_LORA)),
        'mla_w_uk': nrm(13, (N_MLA, KV_LORA, MLA_HEADS * QK_NOPE), KV_LORA ** -0.5),
        'mla_w_uv': nrm(14, (N_MLA, KV_LORA, MLA_HEADS * V_HEAD), KV_LORA ** -0.5),
        'mla_w_o': nrm(15, (N_MLA, MLA_HEADS * V_HEAD, D), (MLA_HEADS * V_HEAD) ** -0.5),
        'hy_w_in': nrm(16, (N_HYENA, D, 3 * D), D ** -0.5),
        'hy_b_in': nrm(17, (N_HYENA, 3 * D), 0.02),
        'hy_conv_w': nrm(18, (N_HYENA, 3, 3 * D), 3 ** -0.5),
        'hy_conv_b': nrm(19, (N_HYENA, 3 * D), 0.02),
        'hy_f_w1': nrm(20, (N_HYENA, HY_POS_DIM, HY_FILTER_HIDDEN), HY_POS_DIM ** -0.5),
        'hy_f_b1': nrm(21, (N_HYENA, HY_FILTER_HIDDEN), 0.1),
        'hy_f_freq1': gain(22, (N_HYENA, HY_FILTER_HIDDEN)),
        'hy_f_w2': nrm(23, (N_HYENA, HY_FILTER_HIDDEN, HY_FILTER_HIDDEN), HY_FILTER_HIDDEN ** -0.5),
        'hy_f_b2': nrm(24, (N_HYENA, HY_FILTER_HIDDEN), 0.1),
        'hy_f_freq2': gain(25, (N_HYENA, HY_FILTER_HIDDEN)),
        'hy_f_w3': nrm(26, (N_HYENA, HY_FILTER_HIDDEN, 2 * D), HY_FILTER_INIT),
        'hy_decay': decay_base[None, :] * (1.0 + nrm(27, (N_HYENA, D), 0.05)),
        'hy_d_bias': nrm(28, (N_HYENA, D), 1.0),
        'hy_w_out': nrm(29, (N_HYENA, D, D), D ** -0.5),
        'hy_b_out': nrm(30, (N_HYENA, D), 0.02),
        'ffn_w_up': nrm(31, (DEPTH, D, 2 * D_FF), D ** -0.5),
        'ffn_conv_w': nrm(32, (DEPTH, 3, 2 * D_FF), 3 ** -0.5),
        'ffn_conv_b': nrm(33, (DEPTH, 2 * D_FF), 0.02),
        'ffn_w_down': nrm(34, (DEPTH, D_FF, D), D_FF ** -0.5),
        'final_g': gain(35, (D,)),
    }

def second_block(x, c, ctx, c_ctx, mod_w, mod_b, norm_mix_g, norm_ffn_g,
              mla_w_dq, mla_g_q, mla_w_uq, mla_w_dkv, mla_g_kv, mla_w_uk, mla_w_uv, mla_w_o,
              hy_w_in, hy_b_in, hy_conv_w, hy_conv_b, hy_f_w1, hy_f_b1, hy_f_freq1, hy_f_w2, hy_f_b2,
              hy_f_freq2, hy_f_w3, hy_decay, hy_d_bias, hy_w_out, hy_b_out,
              ffn_w_up, ffn_conv_w, ffn_conv_b, ffn_w_down, final_g):
    L = x.shape[1]
    ROWS = L // GRID_W
    cos, sin = axial_rope_tables(ROWS)
    silu_c = jax.nn.silu(c)
    silu_cc = jax.nn.silu(c_ctx)
    h_ctx = ctx
    for i in range(DEPTH):
        last = i == DEPTH - 1
        j = i // N_MIXERS
        mod_x = silu_c @ mod_w[i] + mod_b[i]
        mod_c = silu_cc @ mod_w[i] + mod_b[i]
        sh1, sc1, g1, sh2, sc2, g2 = [m[:, None, :] for m in jnp.split(mod_x, 6, axis=-1)]
        csh1, csc1, cg1, csh2, csc2, cg2 = jnp.split(mod_c, 6, axis=-1)
        hx = modulate_2(rmsnorm(x, norm_mix_g[i]), sh1, sc1)
        if i % N_MIXERS == 0:
            hc = modulate_2(rmsnorm(h_ctx, norm_mix_g[i]), csh1, csc1)
            qx = mla_queries(hx, mla_w_dq[j], mla_g_q[j], mla_w_uq[j], cos, sin)
            kx, vx = mla_keys_values(hx, mla_w_dkv[j], mla_g_kv[j], mla_w_uk[j], mla_w_uv[j], cos, sin)
            kc, vc = mla_keys_values(hc, mla_w_dkv[j], mla_g_kv[j], mla_w_uk[j], mla_w_uv[j], None, None)
            ox = block_attention(qx, jnp.concatenate([kc, kx], axis=1), jnp.concatenate([vc, vx], axis=1))
            x = x + g1 * (ox @ mla_w_o[j])
            if not last:
                qc = mla_queries(hc, mla_w_dq[j], mla_g_q[j], mla_w_uq[j], None, None)
                oc = block_attention(qc, kc, vc)
                h_ctx = h_ctx + cg1 * (oc @ mla_w_o[j])
        else:
            hy = (hy_w_in[j], hy_b_in[j], hy_conv_w[j], hy_conv_b[j], hy_f_w1[j], hy_f_b1[j], hy_f_freq1[j],
                  hy_f_w2[j], hy_f_b2[j], hy_f_freq2[j], hy_f_w3[j], hy_decay[j], hy_d_bias[j],
                  hy_w_out[j], hy_b_out[j])
            x = x + g1 * hyena_mixer(hx, *hy)
            if not last:
                hc = modulate_2(rmsnorm(h_ctx, norm_mix_g[i]), csh1, csc1)
                h_ctx = h_ctx + cg1 * hyena_mixer(hc, *hy)
        ffn = (ffn_w_up[i], ffn_conv_w[i], ffn_conv_b[i], ffn_w_down[i])
        x = x + g2 * conv_ffn_2(modulate_2(rmsnorm(x, norm_ffn_g[i]), sh2, sc2), *ffn)
        if not last:
            h_ctx = h_ctx + cg2 * conv_ffn_2(modulate_2(rmsnorm(h_ctx, norm_ffn_g[i]), csh2, csc2), *ffn)
    return rmsnorm(x, final_g)


def setup_inputs(seed=0):
    out = dict(first_inputs(seed))
    for name, value in second_inputs(seed + 1).items():
        if name != "x":
            out[name + "_2"] = value
    return out


def reference(
    x, c, mod_w, mod_b, norm_g, final_g, ab_w_in, ssm_a_re, ssm_a_im, ssm_log_dt, ssm_b_re,
    ssm_b_im, ssm_c_re, ssm_c_im, ssm_d, ssm_glu_w, ssm_glu_b, ab_w_out, rel_bias, cm_w_in,
    cm_b_in, cm_dw_w, cm_dw_b, cm_ln_g, cm_ln_b, cm_w_out, cm_b_out, ffn_w_up, ffn_w_gate,
    ffn_dw_w, ffn_dw_b, ffn_w_down, c_2, ctx_2, c_ctx_2, mod_w_2, mod_b_2, norm_mix_g_2,
    norm_ffn_g_2, mla_w_dq_2, mla_g_q_2, mla_w_uq_2, mla_w_dkv_2, mla_g_kv_2, mla_w_uk_2,
    mla_w_uv_2, mla_w_o_2, hy_w_in_2, hy_b_in_2, hy_conv_w_2, hy_conv_b_2, hy_f_w1_2, hy_f_b1_2,
    hy_f_freq1_2, hy_f_w2_2, hy_f_b2_2, hy_f_freq2_2, hy_f_w3_2, hy_decay_2, hy_d_bias_2,
    hy_w_out_2, hy_b_out_2, ffn_w_up_2, ffn_conv_w_2, ffn_conv_b_2, ffn_w_down_2, final_g_2,
):
    x = first_block(
        x, c, mod_w, mod_b, norm_g, final_g, ab_w_in, ssm_a_re, ssm_a_im, ssm_log_dt, ssm_b_re,
        ssm_b_im, ssm_c_re, ssm_c_im, ssm_d, ssm_glu_w, ssm_glu_b, ab_w_out, rel_bias, cm_w_in,
        cm_b_in, cm_dw_w, cm_dw_b, cm_ln_g, cm_ln_b, cm_w_out, cm_b_out, ffn_w_up, ffn_w_gate,
        ffn_dw_w, ffn_dw_b, ffn_w_down,
    )
    return second_block(
        x, c_2, ctx_2, c_ctx_2, mod_w_2, mod_b_2, norm_mix_g_2, norm_ffn_g_2, mla_w_dq_2,
        mla_g_q_2, mla_w_uq_2, mla_w_dkv_2, mla_g_kv_2, mla_w_uk_2, mla_w_uv_2, mla_w_o_2,
        hy_w_in_2, hy_b_in_2, hy_conv_w_2, hy_conv_b_2, hy_f_w1_2, hy_f_b1_2, hy_f_freq1_2,
        hy_f_w2_2, hy_f_b2_2, hy_f_freq2_2, hy_f_w3_2, hy_decay_2, hy_d_bias_2, hy_w_out_2,
        hy_b_out_2, ffn_w_up_2, ffn_conv_w_2, ffn_conv_b_2, ffn_w_down_2, final_g_2,
    )


_drawn_inputs = setup_inputs


def setup_inputs(seed=0):
    import zlib

    import numpy as np

    out = dict(_drawn_inputs(seed))
    spreads = {}
    factors = {'ctx_2': 8.0,
     'c_ctx_2': 8.0,
     'mod_b_2': 8.0,
     'norm_mix_g_2': 8.0,
     'norm_ffn_g_2': 22.964,
     'mla_w_dq_2': 8.0,
     'mla_g_q_2': 8.0,
     'mla_w_uq_2': 8.0,
     'mla_w_dkv_2': 6.514,
     'mla_g_kv_2': 8.0,
     'mla_w_uk_2': 8.0,
     'mla_w_uv_2': 6.418,
     'mla_w_o_2': 6.906,
     'hy_b_in_2': 8.0,
     'hy_conv_b_2': 8.0,
     'hy_f_b1_2': 4.041,
     'hy_f_freq1_2': 8.0,
     'hy_f_b2_2': 3.249,
     'hy_f_freq2_2': 8.0,
     'hy_decay_2': 4.539,
     'hy_b_out_2': 64.0,
     'ffn_conv_b_2': 61.019}
    for name, (base, spread) in spreads.items():
        noise = np.random.default_rng([zlib.crc32(name.encode()), seed]).standard_normal(out[name].shape)
        drawn = base * np.exp(spread * noise) if base else spread * noise
        out[name] = jnp.asarray(drawn.astype(out[name].dtype))
    for name, factor in factors.items():
        out[name] = (out[name] * factor).astype(out[name].dtype)
    return out
```

```python
from contextlib import ExitStack

import numpy as np

import concourse.bass as bass
from concourse import mybir

F32 = mybir.dt.float32
F32R = mybir.dt.float32r
BF16 = mybir.dt.bfloat16
ALU = mybir.AluOpType
ACT = mybir.ActivationFunctionType
AX_X = mybir.AxisListType.X

STOP = 99

P = 128
T = 256
D = 1024
DT = D // P
F = 2816
FT = F // P
EPS = 1e-6
CHUNK = 2048
SLOTS = 3

SSM_G, SSM_H, SSM_P = 32, 16, 64
ST = SSM_G * SSM_P // P
UT = SSM_G * SSM_H // P
HEADS, HD = 8, 64
TAPS = 31
MH = 16
NOPE, ROPE, VH = 64, 32, 64
QL, KVL = 512, 256
KEYS = 2 * T
HY_HID = 64

MASKED = -1.0e30
MLA_SCALE = float((NOPE + ROPE) ** -0.5)

PAR = [("norm_g", 32), ("mod_b", 96), ("ssm_a_re", 16), ("ssm_a_im", 16),
       ("ssm_d", 4), ("ssm_glu_b", 4), ("ffn_dw_b", 44), ("ffn_dw_w", 132), ("cm_b_in", 16), ("cm_dw_w", 248),
       ("cm_dw_b", 8), ("cm_ln_g", 8), ("cm_ln_b", 8), ("cm_b_out", 8), ("final_g", 8), ("mod_b_2", 96),
       ("norm_mix_g_2", 16), ("norm_ffn_g_2", 16), ("mla_g_q_2", 4), ("mla_g_kv_2", 2), ("hy_b_in_2", 24),
       ("hy_conv_w_2", 72), ("hy_conv_b_2", 24), ("hy_d_bias_2", 8), ("hy_b_out_2", 8), ("ffn_conv_w_2", 264),
       ("ffn_conv_b_2", 88), ("final_g_2", 8)]
COL, _n = {}, 0
for _name, _rows in PAR:
    COL[_name] = _n
    _n += _rows
PAR_ROWS = _n
PAR_T = -(-PAR_ROWS // P)

MOD_COLS = 384
MOD_BLOCKS = 6 * D // MOD_COLS
MOD_SLOTS = 6
MLA_MOD_SLOTS = 2
CTX_COLS = 256
CTX_BLOCKS = 2 * D // CTX_COLS


def consts():
    t = np.arange(T)
    ident = np.eye(P, dtype=np.float32)
    import math
    onehot = np.zeros((33, 2 * T), np.float32)
    for j in range(2 * T - 1):
        d = T - 1 - j
        if d < 0:
            onehot[32, j] = 1.0
            continue
        if d < 16:
            b = d
        else:
            b = 16 + int(np.float32(np.log(np.float32(d) / np.float32(16))) / np.float32(math.log(8.0)) * np.float32(16))
            b = min(b, 31)
        onehot[b, j] = 1.0
    g = (np.arange(P) // SSM_H) % 2
    parity = np.stack([g == 0, g == 1], 1).astype(np.float32)
    half = ROPE // 2
    inv = (np.float32(10000.0) ** (-np.arange(0, half, 2, dtype=np.float32) / np.float32(half))).astype(np.float32)
    row, col = np.repeat(np.arange(T // 64, dtype=np.float32), 64), np.tile(np.arange(64, dtype=np.float32), T // 64)
    ar, ac = row[:, None] * inv, col[:, None] * inv
    ang = np.concatenate([ar, ar, ac, ac], -1).astype(np.float64)
    cos, sin = np.tile(np.cos(ang).T, (4, 1)), np.tile(np.sin(ang).T, (4, 1))
    turn = np.zeros((P, P), np.float32)
    for b in range(0, P, ROPE):
        for i in range(8):
            turn[b + 8 + i, b + i] = -1
            turn[b + i, b + 8 + i] = 1
            turn[b + 24 + i, b + 16 + i] = -1
            turn[b + 16 + i, b + 24 + i] = 1
    w = 2 * np.pi * np.outer(t, np.arange(T) + 0.5) / (2 * T)
    fwd = np.stack([np.cos(w), np.sin(w)]).reshape(2, 2, P, T).transpose(2, 0, 1, 3)
    inv_w = np.stack([np.cos(w.T), np.sin(w.T)]) * (1.0 / T)
    back = inv_w.reshape(2, 2, P, T).transpose(2, 0, 1, 3)
    f32 = np.float32
    lin = np.linspace(0.0, 1.0, T, dtype=f32)
    ww = (f32(2.0 * math.pi) * np.arange(T, dtype=f32) / f32(T)).astype(f32)
    fb = np.linspace(1e-4, 15, 16, dtype=f32)
    arg = (ww[:, None] * fb).astype(f32).astype(np.float64)
    z = np.concatenate([lin[:, None], np.cos(arg), -np.sin(arg)], -1).T
    neg_t = -lin.reshape(2, P).T
    out = dict(ident=ident, onehot=onehot, parity=parity, rope_cos=cos, rope_sin=sin, turn=turn, dft=fwd.reshape(P, 4 * T),
               idft=back.reshape(P, 4 * T), hy_z=z, hy_negt=neg_t)
    return {k: np.ascontiguousarray(v, dtype=np.float32) for k, v in out.items()}


class Count:

    def __init__(self, sem):
        self.sem, self.n = sem, 0

    def on(self, ins):
        ins.then_inc(self.sem, 1)
        self.n += 1
        return self.n


def build(nc, A, out):
    with ExitStack() as ctx:
        def sb(name, shape, dt=F32):
            return ctx.enter_context(nc.sbuf_tensor(name, shape, dt))

        names = {}

        def sem(name):
            if name not in names:
                names[name] = ctx.enter_context(nc.semaphore(name))
            return names[name]

        raw = [sb(f"raw{i}", [P, CHUNK]) for i in range(SLOTS)]
        w_hi = [sb(f"w_hi{i}", [P, CHUNK], F32R) for i in range(SLOTS)]
        w_lo = [sb(f"w_lo{i}", [P, CHUNK], F32R) for i in range(SLOTS)]
        x = sb("x", [P, DT, T])
        h_hi, h_lo = sb("h_hi", [P, DT, T], F32R), sb("h_lo", [P, DT, T], F32R)
        a_hi, a_lo = sb("a_hi", [P, DT, T], F32R), sb("a_lo", [P, DT, T], F32R)
        hf = sb("hf", [P, DT, T])
        sq = sb("sq", [P, DT, T])
        par = sb("par", [P, PAR_T * P])
        mod = sb("mod", [P, 5, 48])
        silu_c = sb("silu_c", [P, 24])
        gains = sb("gains", [P, 2, DT])
        std, rstd = sb("std", [P, T]), sb("rstd", [P, T])
        ident = sb("ident_sb", [P, P])
        ones = sb("ones", [P, P])
        zeros = sb("zeros", [P, 512], BF16)
        eps = sb("eps", [P, 1])
        ARENA = 20480
        arena = sb("arena", [P, ARENA])

        def at(off, *shape):
            n = int(np.prod(shape))
            assert off + n <= ARENA, (off, shape)
            v = arena[:, off:off + n]
            if len(shape) == 2:
                v = v.rearrange("p (a b) -> p a b", a=shape[0])
            if len(shape) == 3:
                v = v.rearrange("p (a b c) -> p a b c", a=shape[0], b=shape[1])
            return v

        HALF = DT // 2 * MOD_COLS
        START_SLOTS = 3
        mod_acc = [at(START_SLOTS * HALF + i * 2 * MOD_COLS, 2, MOD_COLS) for i in range(3)]
        ffn0 = START_SLOTS * HALF + 3 * 2 * MOD_COLS
        gate_c, up_c, gate_s, act_f = (at(ffn0 + 512 * i, 2, T) for i in range(4))
        FREE = ffn0 + 4 * 512
        mod_w = [at((0 if i < START_SLOTS else FREE - START_SLOTS * HALF) + i * HALF, DT // 2, MOD_COLS) for i in range(MOD_SLOTS)]
        xtok = at(ffn0, 2, D)
        out_tok = at(0, 2, D)
        e_re, e_im = at(FREE, ST, T), at(FREE + ST * T, ST, T)
        TAIL = FREE + 2 * ST * T
        par_raw = at(TAIL, PAR_T, P)
        c_rows = at(TAIL + PAR_T * P, P)[0:24, :]
        u_t, q_t, k_t = (at(4 * T * i, UT, T) for i in range(3))
        v_tok = at(3 * 4 * T, 2, HEADS * HD)
        PREP = 4 * 4 * T
        b_nat = at(PREP, 2, ST, SSM_H)
        b_wide = at(PREP + 512, 2, ST, 2 * SSM_H)
        b_tmp = at(PREP + 1536, 2, ST, SSM_H)
        c_nat = at(PREP + 2048, 2, UT, SSM_P)
        c_wide = at(PREP + 2560, 2, UT, P)
        rot_a, rot_b, rot_w = (at(PREP + 512 * i, 2, T) for i in range(3))
        z_buf = [at(PREP + 1536 + 512 * i, 2, T) for i in range(2)]
        s_buf = [at(PREP + 2560 + 512 * i, 2, T) for i in range(2)]
        back_a, back_b = (at(PREP + 3584 + 512 * i, 2, T) for i in range(2))
        b_turned = at(TAIL, 2, UT, P)
        c_turned = at(TAIL + 1024, 2, UT, P)
        y_ssm = at(TAIL + 2048, UT, T)
        hot = at(TAIL + 2048, 2 * T)[0:33, :]
        bias_row = at(TAIL + 2560, 2 * T)[0:HEADS, :]
        padded = at(FREE, DT, T + TAPS - 1)
        sig = at(FREE + DT * (T + TAPS - 1), 2, T)
        mean = at(FREE + DT * (T + TAPS - 1) + 512, T)
        ctx_w = [at(i * DT * CTX_COLS, DT, CTX_COLS) for i in range(3)]
        v_mla = at(0, 2 * KEYS // T, D)
        q_n = at(4096, DT, T)
        c_q = at(6144, QL // P, T)
        c_kv = at(7168, KVL // P, 2, T)
        k_pe = at(8192, 2, T)
        ctx_tok, w_pe_pad = at(FREE, 2, D), None
        ctx_t = at(FREE + 2048, DT, T)
        rope_cos, rope_sin, turn_w = at(FREE + 4096, T), at(FREE + 4352, T), at(FREE + 4608, P)
        k_n = at(FREE + 4992, DT, KEYS)
        mla_mod_w = [at(FREE + i * HALF, DT // 2, MOD_COLS) for i in range(MLA_MOD_SLOTS)]
        mla_mod_acc = [at(FREE + MLA_MOD_SLOTS * HALF + i * 2 * MOD_COLS, 2, MOD_COLS) for i in range(2)]
        q_p, q_raw = at(FREE + 9088, 4, T), at(FREE + 10112, 4, T)
        z_c = at(0, 24, T)
        z_b = [at(6144 + 512 * i, 2, T) for i in range(2)]
        hy_v = at(7168, 2, D)
        hy_s, hy_d = at(9216, 2, D), at(11264, 2, D)
        y_re, y_im = hy_s, hy_d
        f_re, f_im = at(13312, 2, D), at(15360, 2, D)
        decay = at(13312, D)
        dft, idft = at(17408, 2, 2, T), at(18432, 2, 2, T)
        pos = at(19456, T)[0:33, :]
        hid = [at(19712 + T * i, T)[0:HY_HID, :] for i in range(2)]
        hy_w = [at(20224 + HY_HID * i, HY_HID)[0:n, :] for i, n in enumerate((33, HY_HID))]
        angle = [at(11264 + T * i, T)[0:HY_HID, :] for i in range(2)]
        hy_cols = sb("hy_cols", [P, 6])
        cols_ = sb("cols", [P, 23, 16])
        log_dt = sb("log_dt", [P, SSM_G])
        parity = sb("parity_sb", [P, 2])
        tab = sb("tab", [33, HEADS])
        small = sb("small", [P, 32])
        g1b = sb("g1b", [P, DT])

        hy_window = hf[:].rearrange("p (a b) c -> p a (b c)", a=2)
        hy_fwd, hy_bwd = at(15360, D), at(16384, D)
        hy_tmp = at(11264 + 2 * T, T)[0:HY_HID, :]

        def mla_s(h, t):
            return hf[:].rearrange("p (a t b) c -> p a t (b c)", a=2, t=2)[:, h % 2, t, :]

        def mla_p(h):
            return sq[:, 4 * (h % 2):4 * (h % 2) + 4, :]

        def kv_part(v):
            return v[:, 0:4, :].rearrange("p (a b) c -> p a b c", a=2)

        bank = [ctx.enter_context(nc.psum_tensor(f"bank{i}", [P, 512], F32)) for i in range(8)]

        def half(b, e):
            return bank[b][:, e * T:(e + 1) * T]

        W1 = {k: A[k] for k in A}

        def cols(w, c, n):
            return w.rearrange("(k p) n -> p k n", p=P)[:, :, c * n:(c + 1) * n]

        def rows(w, c, n):
            return w[c * n:(c + 1) * n, :].rearrange("(k p) n -> p k n", p=P)

        stream = []
        Q = {}

        def chunks(name, n):
            Q[name] = sum(k for _, k in stream)
            stream.append((name, n))

        chunks("ab_in", 8)
        chunks("glu", 1)
        chunks("ab_out", 4)
        chunks("ffn0", 3 * FT // 2)
        chunks("cm_in", 16 // 2)
        chunks("cm_out", 4)
        chunks("ffn1", 3 * FT // 2)
        chunks("dq", 2)
        chunks("dkv", 2)
        chunks("uq", 3)
        chunks("ukv", 2)
        chunks("mla_out", 4)
        chunks("ffn2", 3 * FT // 2)
        chunks("hy_in", 12)
        chunks("hy_out", 4)
        chunks("ffn3", 3 * FT // 2)
        LAST_FFN = 3
        MB = {0: 0, 1: MOD_BLOCKS, 3: 2 * MOD_BLOCKS, 4: 3 * MOD_BLOCKS}
        NQ = sum(k for _, k in stream)

        FFN = [dict(gate=W1["ffn_w_gate"][i], up=W1["ffn_w_up"][i], down=W1["ffn_w_down"][i]) for i in range(2)]
        FFN += [dict(gate=A["ffn_w_up_gate_2"][i], up=A["ffn_w_up_value_2"][i], down=A["ffn_w_down_2"][i]) for i in range(2)]

        def source(name, c):
            if name == "ab_in":
                return cols(A["ab_w_in"][0], c, 256)
            if name == "glu":
                return cols(A["ssm_glu_w"][0], 0, 512)
            if name == "ab_out":
                return cols(A["ab_w_out"][0], c, 256)
            if name == "cm_in":
                return cols(A["cm_w_in"][0], (c % 2) * 4 + c // 2, 256)
            if name == "cm_out":
                return cols(A["cm_w_out"][0], c, 256)
            if name == "dq":
                return cols(A["mla_w_dq_2"][0], c, 256)
            if name == "dkv" and c == 0:
                return cols(A["mla_w_dkv_2"][0], 0, 256)
            if name == "dkv":
                w = A["mla_w_dkv_2"][0].rearrange("(k p) n -> p k n", p=P)
                return [(slice(None), slice(ROPE * i, ROPE * i + ROPE), w[:, :, KVL:KVL + ROPE]) for i in range(4)] \
                    + [(slice(None), slice(P, 2 * P), w[:, :, 0:P])]
            if name == "uq":
                w = A["mla_w_uq_2"][0].rearrange("(k p) (h c) -> p k h c", p=P, h=MH)
                w = w[:, :, 8 * c:8 * c + 8, 0:NOPE] if c < 2 else w[:, :, :, NOPE:]
                return [(slice(k, k + 1), slice(None), w[:, k]) for k in range(QL // P)]
            if name == "ukv":
                return cols(A[("mla_w_uk_2", "mla_w_uv_2")[c]][0], 0, D)
            if name == "mla_out":
                return cols(A["mla_w_o_2"][0], c, 256)
            if name == "hy_in":
                return cols(A["hy_w_in_2"][0], c, 256)
            if name == "hy_out":
                return cols(A["hy_w_out_2"][0], c, 256)
            raise KeyError(name)

        raw_landed = [sem(f"raw_landed{i}") for i in range(SLOTS)]
        hi_done, lo_done, chunk_done = sem("hi_done"), sem("lo_done"), sem("chunk_done")
        bank_free = sem("bank_free")
        mod_landed = [sem(f"mod_landed{i}") for i in range(MOD_SLOTS)]
        mla_mod_landed = [sem(f"mla_mod_landed{i}") for i in range(MLA_MOD_SLOTS)]
        MOD_HALF, _n_ = [], {}
        for m in range(2 * 4 * MOD_BLOCKS):
            j, stage = m % (2 * MOD_BLOCKS), m // (2 * MOD_BLOCKS)
            n = (START_SLOTS, MOD_SLOTS, MOD_SLOTS, MLA_MOD_SLOTS)[stage]
            buf, landed = ((mla_mod_w, mla_mod_landed) if stage == 3 else (mod_w, mod_landed))
            key = (stage == 3, j % n)
            _n_[key] = _n_.get(key, 0) + 16
            MOD_HALF.append((buf[j % n], landed[j % n], _n_[key], n))

        FILL, _f = {}, 0
        for name, n in (("ab_in", 8), ("glu", 2), ("ab_out", 4), ("ffn0", 0), ("cm_in", 8), ("cm_out", 4), ("ffn1", 0),
                        ("dq", 2), ("dkv", 3), ("uq", 6), ("ukv", 16), ("mla_out", 4), ("ffn2", 0), ("hy_in", 12), ("hy_y", 4),
                        ("hy_out", 4)):
            FILL[name] = _f
            _f += n

        def ffn_columns(f):
            if f < 2:
                return Q[f"ffn{f}"], [COL["ffn_dw_w"] + (3 * f + t) * FT for t in range(3)], None, COL["ffn_dw_b"] + f * FT, None
            w, b = COL["ffn_conv_w_2"] + (f - 2) * 6 * FT, COL["ffn_conv_b_2"] + (f - 2) * 2 * FT
            return Q[f"ffn{f}"], [w + 2 * t * FT + FT for t in range(3)], [w + 2 * t * FT for t in range(3)], b + FT, b

        def steps_before(f, s):
            return not isinstance(s, int) or f + s > 0

        block = ctx.enter_context(nc.Block())

        FFN_INPUT = {0: 2, 1: 5, 2: 11, 3: 13}
        LANDED, _seen = [], [0] * SLOTS
        for name, n in stream:
            for c in range(n):
                src = None if name.startswith("ffn") else source(name, c)
                _seen[len(LANDED) % SLOTS] += 16 * (len(src) if isinstance(src, list) else 1)
                LANDED.append(_seen[len(LANDED) % SLOTS])

        par_pieces = []
        for name, n in PAR:
            src, dims = A[name], " ".join("abcd"[:len(A[name].shape)])
            src = src.rearrange(f"{dims} -> ({dims})") if len(src.shape) > 1 else src
            src = src.rearrange("(r k) -> r k", k=P)
            r = 0
            while r < n:
                row = COL[name] + r
                k = min(n - r, P - row % P)
                par_pieces.append((src[r:r + k, :], par_raw[row % P:row % P + k, row // P, :]))
                r += k

        @block.sync
        def _(sp):
            sp.dma_start(ident[:], A["ident"]).then_inc(sem("ident_landed"), 16)
            for i, name in enumerate(("c", "c_2", "c_ctx_2")):
                src = A[name] if len(A[name].shape) == 1 else A[name].rearrange("a b -> (a b)")
                sp.dma_start(c_rows[8 * i:8 * i + 8, :], src.rearrange("(r k) -> r k", k=P)).then_inc(sem("c_landed"), 16)

            def load(q, src, i=None):
                s = q % SLOTS
                more = 0 if i is None else 6 * i
                if q >= SLOTS:
                    sp.wait_ge(hi_done, q - SLOTS + 1 + more)
                    sp.wait_ge(lo_done, q - SLOTS + 1 + more)
                if not isinstance(src, list):
                    sp.dma_start(raw[s][:].rearrange("p (k n) -> p k n", k=src.shape[1]), src).then_inc(raw_landed[s], 16)
                    return
                kt = D // P if len(src) == 5 else QL // P
                dst = raw[s][:].rearrange("p (k n) -> p k n", k=kt)
                for ks, ns, piece in src:
                    d = dst[:, ks, ns]
                    if len(src) == 4:
                        d = d.rearrange("p o (h c) -> p (o h) c", c=piece.shape[2])
                    sp.dma_start(d, piece).then_inc(raw_landed[s], 16)

            def load_mod(m, w, block_at, kh, i=None):
                more = 0 if i is None else 6 * i
                buf, landed, _, n = MOD_HALF[m]
                if m >= n:
                    sp.wait_ge(sem("mod_used"), m - n + 1 + more)
                src = w.rearrange("(k p) n -> p k n", p=P)[:, kh * 4:(kh + 1) * 4, bass.ds(block_at * MOD_COLS, MOD_COLS)]
                sp.dma_start(buf, src).then_inc(landed, 16)

            def load_ctx_mod(b):
                if b >= 3:
                    sp.wait_ge(sem("ctx_mod_done"), b - 2)
                sp.dma_start(ctx_w[b % 3], cols(A["mod_w_2"][0], b, CTX_COLS)).then_inc(sem(f"ctx_mod_landed{b % 3}"), 16)

            def load_plain(name, c0=0, c1=None):
                for c in range(c0, dict(stream)[name] if c1 is None else c1):
                    load(Q[name] + c, source(name, c))

            def load_ffn(f, mw, b0):
                w, q = FFN[f], Q[f"ffn{f}"]
                load(q, cols(w["gate"], 0, 256))
                load(q + 1, cols(w["up"], 0, 256))
                with sp.Fori(0, 5) as i:
                    for e in range(2):
                        s = 2 * i + 1 + e
                        for j, src in enumerate((w["gate"].rearrange("(k p) n -> p k n", p=P)[:, :, bass.ds(s * 256, 256)],
                                                 w["up"].rearrange("(k p) n -> p k n", p=P)[:, :, bass.ds(s * 256, 256)],
                                                 w["down"].rearrange("(k p) n -> p k n", p=P)[:, bass.ds((s - 1) * 2, 2), :])):
                            load(q + 2 + 3 * e + j, src, i)
                            if mw is not None:
                                if e == j == 0:
                                    sp.wait_ge(sem("h_ready"), FFN_INPUT[f])
                                m = 3 * e + j
                                load_mod(2 * b0 + m, mw, 3 * i + m // 2, m % 2, i)
                load(q + 32, rows(w["down"], FT // 2 - 1, 256))
                if mw is not None:
                    for kh in range(2):
                        load_mod(2 * b0 + 30 + kh, mw, 15, kh)

            for b in range(MOD_BLOCKS):
                for kh in range(2):
                    load_mod(2 * b + kh, A["mod_w"][0], b, kh)
                    if b == kh == 1:
                        sp.dma_start(xtok, A["x"][0].rearrange("(t p) d -> p t d", p=P)).then_inc(sem("x_landed"), 16)
            for c in range(8):
                load(Q["ab_in"] + c, source("ab_in", c))
                if c == 2:
                    sp.wait_ge(sem("mod_turned"), MOD_BLOCKS)
                    for e, n in enumerate(("ssm_b_re", "ssm_b_im")):
                        sp.dma_start(b_nat[:, e], A[n][0].rearrange("(j a) p h -> (a p) j h", a=2)).then_inc(sem("bc_landed"), 16)
                    for e, n in enumerate(("ssm_c_re", "ssm_c_im")):
                        sp.dma_start(c_nat[:, e], A[n][0].rearrange("(t g) h p -> (g h) t p", t=UT)).then_inc(sem("bc_landed"), 16)
            sp.wait_ge(sem("bias_copied"), 16)
            sp.wait_ge(sem("h_ready"), 1)
            for h in range(HEADS):
                if h == 4:
                    load_plain("glu")
                    for c in range(2):
                        load(Q["ab_out"] + c, source("ab_out", c))
                if h >= 4:
                    sp.wait_ge(sem("scores_used"), h - 3)
                for qt in range(2):
                    row = A["bias_copies"][h, 0:1, :]
                    skew = bass.AP(row.tensor, row.offset + T - 1 - qt * P, [[2 * T - 1, P], [1, T]])
                    sp.dma_start(sq[:, 2 * (h % 4) + qt, :], skew).then_inc(sem(f"bias_back{h // 4}"), 16)
            for c in range(2, 4):
                load(Q["ab_out"] + c, source("ab_out", c))
            load_ffn(0, A["mod_w"][1], MB[1])
            load_plain("cm_in", 0, 3)
            sp.wait_ge(sem("mod_turned"), MB[1] + MOD_BLOCKS)
            sp.wait_ge(sem("x_ready"), 2)
            for b in range(3):
                load_ctx_mod(b)
            load_plain("cm_in", 3)
            load_plain("cm_out", 0, 2)
            for b in range(3, CTX_BLOCKS):
                load_ctx_mod(b)
            load_plain("cm_out", 2)
            load_ffn(1, A["mod_w_2"][0], MB[3])
            for name in ("dq", "dkv"):
                load_plain(name)
                if name == "dq":
                    sp.wait_ge(sem("mod_used"), 2 * MB[4])
                    sp.dma_start(ctx_tok, A["ctx_2"][0].rearrange("(t p) d -> p t d", p=P)).then_inc(sem("ctx_landed"), 16)
                    for n, dst in (("rope_cos", rope_cos), ("rope_sin", rope_sin), ("turn", turn_w)):
                        sp.dma_start(dst, A[n]).then_inc(sem("rope_landed"), 16)
            for name in ("uq", "ukv", "mla_out"):
                load_plain(name)
            sp.wait_ge(sem("q_pe_ready"), 1)
            for b in range(MOD_BLOCKS):
                for kh in range(2):
                    load_mod(2 * (MB[4] + b) + kh, A["mod_w_2"][1], b, kh)
            load_ffn(2, None, None)
            load_plain("hy_in", 0, 3)
            for n, dst in (("dft", dft), ("idft", idft)):
                sp.dma_start(dst, A[n].rearrange("p (a b t) -> p a b t", a=2, b=2)).then_inc(sem("hy_landed"), 16)
            sp.dma_start(pos, A["hy_z"]).then_inc(sem("hy_landed"), 16)
            sp.dma_start(hy_w[0], A["hy_f_w1_2"][0]).then_inc(sem("hy_landed"), 16)
            sp.dma_start(hy_w[1], A["hy_f_w2_2"][0]).then_inc(sem("hy_landed"), 16)
            for i, n in enumerate(("hy_f_b1_2", "hy_f_freq1_2", "hy_f_b2_2", "hy_f_freq2_2")):
                sp.dma_start(hy_cols[0:HY_HID, i:i + 1], A[n].rearrange("a k -> k a")).then_inc(sem("hy_landed"), 16)
            sp.dma_start(hy_cols[:, 4:6], A["hy_negt"]).then_inc(sem("hy_landed"), 16)
            sp.dma_start(decay, A["hy_decay_2"][0].partition_broadcast(P)).then_inc(sem("hy_landed"), 16)
            sp.wait_ge(sem("h_ready"), 12)
            sp.dma_start(sq[0:HY_HID].rearrange("p a b -> p (a b)"), A["hy_f_w3_2"][0]).then_inc(sem("hy_w3_landed"), 16)
            load_plain("hy_in", 3, 12)
            load_plain("hy_out")
            load_ffn(3, None, None)
            for t in range(2):
                sp.wait_ge(sem("out_turned"), t + 1)
                sp.dma_start(out[t * P:(t + 1) * P, :], out_tok[:, t, :]).then_inc(sem("stored"), 16)
            sp.wait_ge(sem("stored"), 32)

        @block.gpsimd
        def _(pool):
            done = Count(sem("pool_chain"))

            def link(ins):
                pool.wait_ge(done.sem, done.on(ins))

            pool.wait_ge(sem("theta_ready"), 1)
            pr, pi, qr, qi, t0, t1 = (cols_[:, i, :] for i in range(12, 18))
            m = 1
            for step in range(8):
                a, b = hf[:].rearrange("p a b -> p (a b)")[:, 0:ST * m].rearrange("p (a b) -> p a b", a=ST), \
                    sq[:].rearrange("p a b -> p (a b)")[:, 0:ST * m].rearrange("p (a b) -> p a b", a=ST)
                br, bi = (v.unsqueeze(2).broadcast_to([P, ST, m]) for v in (pr, pi))
                lo, up = slice(0, m), slice(m, 2 * m)
                nc.gpsimd.tensor_tensor(a, e_re[:, :, lo], br, ALU.mult)
                link(nc.gpsimd.tensor_tensor(b, e_im[:, :, lo], bi, ALU.mult))
                link(nc.gpsimd.tensor_tensor(e_re[:, :, up], a, b, ALU.subtract))
                nc.gpsimd.tensor_tensor(a, e_re[:, :, lo], bi, ALU.mult)
                link(nc.gpsimd.tensor_tensor(b, e_im[:, :, lo], br, ALU.mult))
                link(nc.gpsimd.tensor_tensor(e_im[:, :, up], a, b, ALU.add))
                nc.gpsimd.tensor_tensor(qr, pr, pr, ALU.mult)
                nc.gpsimd.tensor_tensor(qi, pi, pi, ALU.mult)
                link(nc.gpsimd.tensor_tensor(t0, pr, pi, ALU.mult))
                nc.gpsimd.tensor_tensor(pr, qr, qi, ALU.subtract)
                link(nc.gpsimd.tensor_tensor(pi, t0, t0, ALU.add))
                m *= 2
            nc.gpsimd.tensor_copy(t1, t0).then_inc(sem("e_ready"), 1)

            for j in range(ST):
                pool.wait_ge(sem("scan_done"), j + 1)
                if j >= 1:
                    pool.wait_ge(sem("state_ready"), j)
                if j >= 2:
                    pool.wait_ge(sem("ssm_y_done"), j - 1)
                z, s_ = z_buf[j % 2], s_buf[j % 2]
                nc.gpsimd.tensor_tensor(back_a, z, e_re[:, j, :].unsqueeze(1).broadcast_to([P, 2, T]), ALU.mult)
                link(nc.gpsimd.tensor_tensor(back_b, z, e_im[:, j, :].unsqueeze(1).broadcast_to([P, 2, T]), ALU.mult))
                nc.gpsimd.tensor_tensor(s_[:, 0, :], back_a[:, 0, :], back_b[:, 1, :], ALU.subtract)
                nc.gpsimd.tensor_tensor(s_[:, 1, :], back_a[:, 1, :], back_b[:, 0, :], ALU.add).then_inc(sem("state_ready"), 1)

        @block.scalar
        def _(act):
            nxt = [0]

            def hi(q, i=None):
                s = q % SLOTS
                act.wait_ge(raw_landed[s], LANDED[q] + (0 if i is None else 32 * i))
                if q >= SLOTS:
                    act.wait_ge(chunk_done, q - SLOTS + 1 + (0 if i is None else 6 * i))
                nc.scalar.activation(w_hi[s][:], raw[s][:], ACT.Copy).then_inc(hi_done, 1)

            def hi_upto(q):
                while nxt[0] <= min(q, NQ - 1):
                    hi(nxt[0])
                    nxt[0] += 1

            def norm_parts(n, src, kt, width):
                nc.scalar.activation(sq[:, 0:kt, :], src, ACT.Square).then_inc(sem("sq_ready"), 1)
                act.wait_ge(sem("norm_sum"), n + 1)
                if n:
                    act.wait_ge(sem("rstd_ready"), n)
                nc.scalar.activation(std[:], bank[7][:, 0:T], ACT.Sqrt, bias=eps[:, 0:1], scale=1.0 / width)\
                    .then_inc(sem("std_ready"), 1)

            act.wait_ge(sem("c_turned"), 1)
            nc.scalar.activation(silu_c[:], bank[7][:, 0:24], ACT.Silu).then_inc(sem("silu_c_ready"), 1)
            for src, dst in par_pieces:
                act.dma_start(dst, src).then_inc(sem("par_landed"), 16)
            act.dma_start(log_dt[:], A["ssm_log_dt"][0].partition_broadcast(P)).then_inc(sem("log_dt_landed"), 16)
            act.dma_start(tab[0:32, :], A["rel_bias"]).then_inc(sem("tab_landed"), 16)
            act.dma_start(tab[32:33, :], A["masked"]).then_inc(sem("tab_landed"), 16)
            act.dma_start(hot, A["onehot"]).then_inc(sem("tab_landed"), 16)
            act.dma_start(parity[:], A["parity"]).then_inc(sem("parity_landed"), 16)
            act.wait_ge(sem("log_dt_landed"), 16)
            ld = log_dt[:].rearrange("p (j a) -> p j a", a=2)
            for a in range(2):
                ins = nc.scalar.activation(cols_[64 * a:64 * a + 64, 0, :], ld[64 * a:64 * a + 64, :, a], ACT.Exp)
            ins.then_inc(sem("dt_ready"), 1)
            act.wait_ge(sem("decay_ready"), 1)
            nc.scalar.activation(cols_[:, 2, :], cols_[:, 1, :], ACT.Exp).then_inc(sem("mag_ready"), 1)
            act.wait_ge(sem("angle_ready"), 1)
            nc.scalar.activation(cols_[:, 8:10, :], cols_[:, 6:8, :], ACT.Sin).then_inc(sem("sin_ready"), 1)
            act.wait_ge(sem("bias_row_ready"), 1)
            act.dma_start(A["bias_row"], bias_row).then_inc(sem("bias_out"), 16)
            hi_upto(2)
            act.wait_ge(sem("bias_out"), 16)
            act.dma_start(A["bias_copies"], A["bias_row"].unsqueeze(1).broadcast_to([HEADS, P, 2 * T])).then_inc(sem("bias_copied"), 16)

            act.wait_ge(sem("e_ready"), 1)
            act.wait_ge(sem("x_ready"), 1)
            norm_parts(0, x[:], DT, D)
            for c in range(8):
                q = Q["ab_in"] + c
                act.wait_ge(chunk_done, q + 1)
                src = bank[4 + (FILL["ab_in"] + c) % 2][:].rearrange("p (a b) -> p a b", a=2)
                if c < 6:
                    dst = (u_t, q_t, k_t)[c // 2][:, (c % 2) * 2:(c % 2) * 2 + 2, :]
                else:
                    dst = v_tok[:, :, (c - 6) * 256:(c - 5) * 256]
                if c == 0:
                    act.wait_ge(sem("mod_used"), 2 * MOD_BLOCKS)
                    act.wait_ge(sem("mod_turned"), MOD_BLOCKS)
                nc.scalar.activation(dst, src, ACT.Copy).then_inc(bank_free, 1)
                hi_upto(q + 3)

            sT = hf[:].rearrange("p (b c) t -> p b c t", c=2)
            pT = [hf[:, 4 + 2 * i:6 + 2 * i, :] for i in range(2)]
            for h in range(HEADS):
                act.wait_ge(sem("peak_ready"), h + 1)
                for qt in range(2):
                    s = hf[:, 2 * (h % 2) + qt, :]
                    k = 4 * (h % 2) + qt
                    ins = nc.scalar.activation(s, s, ACT.Exp, bias=small[:, k:k + 1], accum_out=small[:, k + 2:k + 3])
                ins.then_inc(sem("exp_ready"), 1)
                act.wait_ge(sem("probs_turned"), h + 1)
                nc.scalar.activation(pT[h % 2], bank[6][:].rearrange("p (a b) -> p a b", a=2), ACT.Copy).then_inc(sem("probs_t"), 1)
                act.wait_ge(sem("head_done"), h + 1)
                r = 64 * (h % 2)
                nc.scalar.activation(q_t[r:r + 64, h // 2, :], bank[7][r:r + 64, 0:T], ACT.Copy).then_inc(sem("att_out"), 1)
            for n in range(UT):
                act.wait_ge(sem("y_ready"), n + 1)
                nc.scalar.activation(y_ssm[:, n, :], y_ssm[:, n, :], ACT.Gelu_apprx_tanh).then_inc(sem("gelu_done"), 1)
            q = Q["glu"]
            act.wait_ge(sem("gelu_done"), UT)
            nc.scalar.activation(a_hi[:, 0:UT, :], y_ssm, ACT.Copy).then_inc(sem("part_hi"), 1)
            act.wait_ge(chunk_done, q + 1)
            for n in range(UT):
                c0 = COL["ssm_glu_b"] + n
                ins = nc.scalar.activation(u_t[:, n, :], half(4 + n // 2, n % 2), ACT.Sigmoid, bias=par[:, c0:c0 + 1])
                if n % 2:
                    ins.then_inc(bank_free, 1)
            hi_upto(q + 3)
            act.wait_ge(sem("ssm_out"), 1)
            nc.scalar.activation(h_hi[:, 0:UT, :], u_t, ACT.Copy)
            act.wait_ge(sem("att_out"), HEADS)
            nc.scalar.activation(h_hi[:, UT:, :], q_t, ACT.Copy).then_inc(sem("part_hi"), 1)
            for c in range(4):
                hi_upto(Q["ab_out"] + c + 3)
            act.wait_ge(bank_free, FILL["ab_out"] + 4)
            norm_parts(1, x[:], DT, D)

            def ffn(f):
                last, two = f == LAST_FFN, f >= 2
                q0, wb, wu, bb, bu_ = ffn_columns(f)
                center = 1 if two else 2
                done = f * (FT // 2)

                def step(s, q, i=None):
                    more = 0 if i is None else 6 * i
                    steps = done + s
                    act.wait_ge(chunk_done, q + 1 + more)
                    for e in range(2):
                        ins = nc.scalar.activation(gate_c[:, e, :], half(4, e), ACT.Identity,
                                                   scale=par[:, bass.ds(wb[center] + 2 * s + e, 1)],
                                                   bias=par[:, bass.ds(bb + 2 * s + e, 1)])
                    ins.then_inc(sem("tap_ready"), 1)
                    yield
                    if two:
                        act.wait_ge(chunk_done, q + 2 + more)
                        if steps_before(f, s):
                            act.wait_ge(sem("act_ready"), steps)
                        for e in range(2):
                            ins = nc.scalar.activation(up_c[:, e, :], half(5, e), ACT.Identity,
                                                       scale=par[:, bass.ds(wu[center] + 2 * s + e, 1)],
                                                       bias=par[:, bass.ds(bu_ + 2 * s + e, 1)])
                        ins.then_inc(sem("up_tap_ready"), 1)
                    act.wait_ge(sem("conv_done"), steps + 1)
                    nc.scalar.activation(gate_s, gate_c, ACT.Silu).then_inc(sem("silu_ready"), 1)
                    yield
                    act.wait_ge(sem("act_ready"), steps + 1)
                    nc.scalar.activation(slot_hi(q), act_f, ACT.Copy)\
                        .then_inc(sem("act_hi"), 1)
                    yield

                def slot_hi(q):
                    k = 2 * (((q - q0 + 1) // 3) % 2)
                    return a_hi[:, k:k + 2, :]

                def run(s, q, nq, i=None):
                    g = step(s, q, i)
                    for k in range(3):
                        next(g)
                        if nq + k < NQ or i is not None:
                            hi(nq + k, i)

                g = step(0, q0)
                next(g)
                hi(q0 + 3)
                next(g)
                hi(q0 + 4)
                next(g)
                if last:
                    turns = 4
                else:
                    turns = 5
                with act.Fori(0, turns) as i:
                    run(2 * i + 1, q0 + 2, q0 + 5, i)
                    run(2 * i + 2, q0 + 5, q0 + 8, i)
                if last:
                    run(9, q0 + 26, q0 + 29)
                    run(10, q0 + 29, q0 + 32)
                nxt[0] = q0 + 35
                hi_upto(q0 + 35)

            ffn(0)

            act.wait_ge(sem("x_ready"), 2)
            norm_parts(2, x[:], DT, D)
            for p in range(4):
                q, fill = Q["cm_in"] + 2 * p, FILL["cm_in"] + 2 * p
                hi_upto(q + 3)
                act.wait_ge(chunk_done, q + 2)
                if p:
                    act.wait_ge(bank_free, fill)
                for e in range(2):
                    c0 = COL["cm_b_in"] + DT + 2 * p + e
                    ins = nc.scalar.activation(sig[:, e, :], half(4 + (fill + 1) % 2, e), ACT.Sigmoid, bias=par[:, c0:c0 + 1])
                ins.then_inc(sem("sig_ready"), 1)
                hi_upto(q + 4)
            act.wait_ge(sem("centered"), 1)
            norm_parts(3, hf[:], DT, D)
            act.wait_ge(sem("ln_ready"), 1)
            for k in range(DT):
                g, b = COL["cm_ln_g"] + k, COL["cm_ln_b"] + k
                ins = nc.scalar.activation(hf[:, k, :], hf[:, k, :], ACT.Silu, scale=par[:, g:g + 1], bias=par[:, b:b + 1])
            ins.then_inc(sem("ln_silu"), 1)
            for c in range(4):
                hi_upto(Q["cm_out"] + c + 3)
            act.wait_ge(bank_free, FILL["cm_out"] + 4)
            norm_parts(4, x[:], DT, D)
            ffn(1)
            act.wait_ge(sem("x_ready"), 3)
            norm_parts(5, x[:], DT, D)

            act.wait_ge(sem("x_ready"), 4)
            norm_parts(6, x[:], DT, D)
            act.wait_ge(sem("ctx_ready"), 1)
            norm_parts(7, ctx_t, DT, D)

            def evacuate(name, n, dst):
                fill = FILL[name] + n
                nc.scalar.activation(dst, bank[4 + fill % 2][:].rearrange("p (a b) -> p a b", a=2), ACT.Copy).then_inc(bank_free, 1)

            for c in range(2):
                act.wait_ge(chunk_done, Q["dq"] + c + 1)
                evacuate("dq", c, c_q[:, 2 * c:2 * c + 2, :])
                hi_upto(Q["dq"] + c + 3)
            act.wait_ge(chunk_done, Q["dkv"] + 1)
            for n in range(2):
                evacuate("dkv", n, c_kv[:, n])
            hi_upto(Q["dkv"] + 3)
            act.wait_ge(chunk_done, Q["dkv"] + 2)
            evacuate("dkv", 2, k_pe)
            act.wait_ge(bank_free, FILL["dkv"] + 3)
            norm_parts(8, c_q, QL // P, QL)
            for e in range(2):
                norm_parts(9 + e, c_kv[:, :, e, :], KVL // P, KVL)
            hi_upto(Q["dkv"] + 4)
            for c in range(3):
                act.wait_ge(chunk_done, Q["uq"] + c + 1)
                for n in range(2):
                    t = 4 * c + 2 * n
                    evacuate("uq", 2 * c + n, q_n[:, t:t + 2, :] if c < 2 else q_raw[:, 2 * n:2 * n + 2, :])
                hi_upto(Q["uq"] + c + 3)
            def kv_ready(n):
                if n % 8 == 7:
                    act.wait_ge(chunk_done, Q["ukv"] + n // 8 + 1)
                else:
                    act.wait_ge(sem("kv_filled"), n + 1 - n // 8)

            for n in range(8):
                kv_ready(n)
                evacuate("ukv", n, k_n[:, n, :].rearrange("p (a b) -> p a b", a=2))
            hi_upto(Q["ukv"] + 3)
            for n in range(8):
                kv_ready(8 + n)
                evacuate("ukv", 8 + n, v_mla[:, n // 2, (n % 2) * 512:(n % 2) * 512 + 512].rearrange("p (a b) -> p a b", a=2))
            hi_upto(Q["ukv"] + 4)

            def mla_exp(h):
                for t in range(2):
                    u = 2 * h + t
                    act.wait_ge(sem("mla_peak"), u + 1)
                    if h >= 2:
                        act.wait_ge(sem("mla_turned"), h - 1)
                    k = 8 * (h % 2) + 4 * t
                    nc.scalar.activation(mla_s(h, t), bank[u % 4][:], ACT.Exp, bias=small[:, k + 1:k + 2], scale=MLA_SCALE,
                                         accum_out=small[:, k + 2:k + 3]).then_inc(sem("mla_exp"), 1)

            mla_exp(0)
            for h in range(MH):
                if h + 1 < MH:
                    mla_exp(h + 1)
                act.wait_ge(sem("mla_turned"), h + 1)
                if h >= 2:
                    act.wait_ge(sem("mla_head"), h - 1)
                nc.scalar.activation(mla_p(h)[:, 0:2, :], bank[4][:].rearrange("p (a b) -> p a b", a=2), ACT.Copy).then_inc(sem("mla_pt0"), 1)
                act.wait_ge(sem("mla_head"), h + 1)
                r = 64 * (h % 2)
                nc.scalar.activation(q_n[r:r + 64, h // 2, :], bank[7][r:r + 64, 0:T], ACT.Copy).then_inc(sem("mla_out"), 1)
            act.wait_ge(sem("mla_out"), MH)
            nc.scalar.activation(h_hi[:], q_n, ACT.Copy).then_inc(sem("part_hi"), 1)
            for c in range(4):
                hi_upto(Q["mla_out"] + c + 3)
            act.wait_ge(bank_free, FILL["mla_out"] + 4)
            norm_parts(11, x[:], DT, D)
            ffn(2)

            act.wait_ge(sem("x_ready"), 5)
            norm_parts(12, x[:], DT, D)
            for c in range(12):
                q, fill = Q["hy_in"] + c, FILL["hy_in"] + c
                act.wait_ge(chunk_done, q + 1)
                if c >= 2:
                    act.wait_ge(sem("hy_conv"), c - 1)
                for e in range(2):
                    c0 = COL["hy_b_in_2"] + 2 * c + e
                    ins = nc.scalar.activation(z_b[c % 2][:, e, :], half(4 + fill % 2, e), ACT.Identity, bias=par[:, c0:c0 + 1])
                ins.then_inc(bank_free, 1)
                hi_upto(q + 3)
                if c < 2:
                    act.wait_ge(sem("hy_angle"), c + 1)
                    nc.scalar.activation(hid[c], angle[0], ACT.Sin).then_inc(sem("hy_hid"), 1)
                elif c < 4:
                    t = c - 2
                    if t == 0:
                        nc.scalar.activation(decay, decay, ACT.Abs).then_inc(sem("hy_decay"), 1)
                        act.wait_ge(sem("hy_decay"), 1)
                    nc.scalar.activation(hy_window[:, t, :], decay, ACT.Exp, scale=hy_cols[:, 4 + t:5 + t]).then_inc(sem("hy_window"), 1)
                elif c < 6:
                    hf_ = c - 4
                    act.wait_ge(sem("filter_done"), hf_ + 1)
                    for part, dst in enumerate((f_re, f_im)):
                        for ft in range(2):
                            ins = nc.scalar.activation(dst[:, ft, 512 * hf_:512 * hf_ + 512], bank[2 * part + ft][:], ACT.Copy)
                    ins.then_inc(sem("filter_ready"), 1)
            for c in range(4):
                act.wait_ge(sem("v_turned"), c + 1)
                nc.scalar.activation(hy_v[:, :, 256 * c:256 * c + 256], bank[6 + c % 2][:].rearrange("p (a b) -> p a b", a=2), ACT.Copy)\
                    .then_inc(sem("hy_v_ready"), 1)
            act.wait_ge(sem("hy_y_ready"), 4)
            nc.scalar.activation(h_hi[:], z_c[:, DT:2 * DT, :], ACT.Copy).then_inc(sem("part_hi"), 1)
            for c in range(4):
                hi_upto(Q["hy_out"] + c + 3)
            act.wait_ge(bank_free, FILL["hy_out"] + 4)
            norm_parts(13, x[:], DT, D)
            ffn(3)
            act.wait_ge(sem("x_ready"), 6)
            norm_parts(14, x[:], DT, D)

        @block.vector
        def _(dve):
            chain = Count(sem("dve_chain"))

            def link(ins):
                dve.wait_ge(chain.sem, chain.on(ins))

            nxt = [0]

            def lo(q, i=None):
                s = q % SLOTS
                dve.wait_ge(hi_done, q + 1 + (0 if i is None else 6 * i))
                nc.vector.tensor_tensor(w_lo[s][:], raw[s][:], w_hi[s][:].bitcast(F32), ALU.subtract).then_inc(lo_done, 1)

            def lo_upto(q):
                while nxt[0] <= min(q, NQ - 1):
                    lo(nxt[0])
                    nxt[0] += 1

            nc.vector.memset(ones[:], 1.0)
            nc.vector.memset(eps[:], EPS)
            nc.vector.memset(zeros[:], 0.0).then_inc(sem("const_ready"), 1)
            def mod_block(b, c0, i=None):
                per = 0 if i is None else i
                ring = mla_mod_acc if b >= MB[4] else mod_acc
                acc = ring[b % len(ring)]
                if b >= len(ring):
                    dve.wait_ge(sem("mod_turned"), b - len(ring) + 1 + 3 * per)
                last = [None, None]
                for kt in range(DT):
                    kh, e = kt // 4, kt % 2
                    buf, landed, n, _ = MOD_HALF[2 * b + kh]
                    w = buf[:, kt % 4, :]
                    c = silu_c[:, c0 + kt:c0 + kt + 1]
                    if kt % 4 == 0:
                        dve.wait_ge(landed, n + 16 * per)
                    if kt < 2:
                        ins = nc.vector.tensor_scalar(acc[:, e, :], w, c, None, ALU.mult)
                    else:
                        if last[e] is None:
                            dve.wait_ge(sem("mod_used"), 2 * b + 1 + 6 * per)
                        else:
                            chain_wait(last[e])
                        ins = nc.vector.scalar_tensor_tensor(acc[:, e, :], w, c, acc[:, e, :], ALU.mult, ALU.add)
                    if kt % 4 == 3:
                        ins.then_inc(sem("mod_used"), 1)
                        last[e] = None
                    else:
                        last[e] = chain.on(ins)

            more = [0]

            def chain_wait(n):
                dve.wait_ge(chain.sem, n + more[0])

            dve.wait_ge(sem("silu_c_ready"), 1)
            for b in range(4):
                mod_block(b, 0)
            for t in range(3):
                n = min(512, PAR_ROWS - 512 * t)
                dve.wait_ge(sem("par_turned"), t + 1)
                nc.vector.tensor_copy(par[:, 512 * t:512 * t + n], bank[t][:, 0:n]).then_inc(sem("par_ready"), 1)
            dve.wait_ge(sem("par_ready"), 3)
            dt, dec, mag, th, k_, r_ = (cols_[:, i, :] for i in range(6))
            sin_in, sn, cs = cols_[:, 6:8, :], cols_[:, 8, :], cols_[:, 9, :]
            abr, abi, den, n0, n1, cr, ci = (cols_[:, i, :] for i in (10, 11, 18, 19, 20, 21, 22))
            lr, li = (par[:, COL[n]:COL[n] + ST] for n in ("ssm_a_re", "ssm_a_im"))
            dve.wait_ge(sem("dt_ready"), 1)
            nc.vector.tensor_tensor(dec, lr, dt, ALU.mult).then_inc(sem("decay_ready"), 1)
            link(nc.vector.tensor_tensor(th, li, dt, ALU.mult))

            def reduce_angle(dst, src, tmp):
                two_pi = 2 * np.pi
                hi_ = 6.28125
                mid = float(np.float32(np.round((two_pi - hi_) * 2 ** 20) / 2 ** 20))
                low = two_pi - hi_ - mid
                magic = 1.5 * 2 ** 23
                link(nc.vector.tensor_scalar(tmp, src, float(1 / two_pi), magic, ALU.mult, ALU.add))
                link(nc.vector.tensor_scalar(tmp, tmp, magic, None, ALU.subtract))
                link(nc.vector.scalar_tensor_tensor(dst, tmp, -hi_, src, ALU.mult, ALU.add))
                link(nc.vector.scalar_tensor_tensor(dst, tmp, -mid, dst, ALU.mult, ALU.add))
                link(nc.vector.scalar_tensor_tensor(dst, tmp, -low, dst, ALU.mult, ALU.add))
                pi = float(np.float32(3.1415925))
                return nc.vector.tensor_scalar(dst, dst, pi, -pi, ALU.min, ALU.max)

            link(reduce_angle(cols_[:, 6, :], th, k_))
            link(nc.vector.tensor_scalar(r_, cols_[:, 6, :], float(np.pi / 2), None, ALU.add))
            reduce_angle(cols_[:, 7, :], r_, k_).then_inc(sem("angle_ready"), 1)
            dve.wait_ge(sem("sin_ready"), 1)
            dve.wait_ge(sem("mag_ready"), 1)
            nc.vector.memset(e_re[:, :, 0:1], 1.0)
            nc.vector.memset(e_im[:, :, 0:1], 0.0)
            nc.vector.tensor_copy(cols_[:, 12, :], cs)
            nc.vector.tensor_copy(cols_[:, 13, :], sn).then_inc(sem("theta_ready"), 1)
            nc.vector.tensor_tensor(abr, mag, cs, ALU.mult)
            link(nc.vector.tensor_tensor(abi, mag, sn, ALU.mult))
            nc.vector.tensor_tensor(n0, lr, lr, ALU.mult)
            link(nc.vector.tensor_tensor(n1, li, li, ALU.mult))
            link(nc.vector.tensor_tensor(den, n0, n1, ALU.add))
            link(nc.vector.reciprocal(den, den))
            link(nc.vector.tensor_scalar(abr, abr, -1.0, None, ALU.add))
            nc.vector.tensor_tensor(n0, abr, lr, ALU.mult)
            link(nc.vector.tensor_tensor(n1, abi, li, ALU.mult))
            link(nc.vector.tensor_tensor(cr, n0, n1, ALU.add))
            link(nc.vector.tensor_tensor(cr, cr, den, ALU.mult))
            nc.vector.tensor_tensor(n0, abi, lr, ALU.mult)
            link(nc.vector.tensor_tensor(n1, abr, li, ALU.mult))
            link(nc.vector.tensor_tensor(ci, n0, n1, ALU.subtract))
            link(nc.vector.tensor_tensor(ci, ci, den, ALU.mult))
            dve.wait_ge(sem("bias_row_done"), 1)
            nc.vector.tensor_copy(bias_row, bank[7][0:HEADS, :]).then_inc(sem("bias_row_ready"), 1)
            for b in range(4):
                dve.wait_ge(sem("x_turned"), b + 1)
                ins = nc.vector.tensor_copy(x[:, 2 * b:2 * b + 2, :], bank[b][:].rearrange("p (a b) -> p a b", a=2))
            ins.then_inc(sem("x_ready"), 1)

            def mod_out(l, b, name, row):
                dve.wait_ge(sem("mod_turned"), b)
                link(nc.vector.tensor_tensor(mod[:, l, :], bank[6][:, 0:48], par[:, COL[name] + row:COL[name] + row + 48], ALU.add))

            for b in range(4, MOD_BLOCKS):
                mod_block(b, 0)
            mod_out(0, MOD_BLOCKS, "mod_b", 0)

            def gain(g, sc):
                link(nc.vector.scalar_tensor_tensor(gains[:, 0, :], sc, 1.0, g, ALU.add, ALU.mult))

            def norm(n, src, kt, scale, shift, hi_, lo_):
                dve.wait_ge(sem("std_ready"), n + 1)
                nc.vector.reciprocal(rstd[:], std[:]).then_inc(sem("rstd_ready"), 1)
                dve.wait_ge(sem("rstd_ready"), n + 1)
                link(nc.vector.tensor_tensor(hf[:, 0:kt, :], src, rstd[:].unsqueeze(1).broadcast_to([P, kt, T]), ALU.mult))
                for k in range(kt):
                    ins = nc.vector.tensor_scalar(hf[:, k, :], hf[:, k, :], scale(k), shift(k), ALU.mult, ALU.add)
                link(ins)
                link(nc.vector.tensor_copy(hi_, hf[:, 0:kt, :]))
                nc.vector.tensor_tensor(lo_, hf[:, 0:kt, :], hi_.bitcast(F32), ALU.subtract).then_inc(sem("h_ready"), 1)

            lo_upto(2)
            gain(par[:, COL["norm_g"]:COL["norm_g"] + 8], mod[:, 0, 8:16])
            norm(0, x[:], DT, lambda k: gains[:, 0, k:k + 1], lambda k: mod[:, 0, k:k + 1], h_hi[:], h_lo[:])
            for c in range(8):
                lo_upto(Q["ab_in"] + c + 3)
                if c == 0:
                    dve.wait_ge(sem("bc_landed"), 64)
                    dve.wait_ge(sem("parity_landed"), 16)
                    crb, cib = (v.unsqueeze(2).broadcast_to([P, ST, SSM_H]) for v in (cr, ci))
                    br, bi = b_nat[:, 0], b_nat[:, 1]
                    link(nc.vector.memset(b_wide, 0.0))
                    for e, (p0, p1, op) in enumerate(((br, bi, ALU.subtract), (bi, br, ALU.add))):
                        nc.vector.tensor_tensor(b_tmp[:, 0], p0, crb, ALU.mult)
                        link(nc.vector.tensor_tensor(b_tmp[:, 1], p1, cib, ALU.mult))
                        for a in range(2):
                            r = slice(64 * a, 64 * a + 64)
                            ins = nc.vector.tensor_tensor(b_wide[r, e, :, SSM_H * a:SSM_H * a + SSM_H], b_tmp[r, 0], b_tmp[r, 1], op)
                        link(ins)
                    for e, sign in ((0, 1.0), (1, -1.0)):
                        for a in range(2):
                            ins = nc.vector.tensor_scalar(c_wide[:, e, :, SSM_P * a:SSM_P * a + SSM_P], c_nat[:, e], parity[:, a:a + 1],
                                                          sign, ALU.mult, ALU.mult)
                    ins.then_inc(sem("bc_wide"), 1)
                    for b, dst in enumerate((b_turned, c_turned)):
                        for e in range(2):
                            dve.wait_ge(sem("bc_turned"), 2 * b + e + 1)
                            ins = nc.vector.tensor_copy(dst[:, e], bank[2 * b + e][:].rearrange("p (a b) -> p a b", a=UT))
                    ins.then_inc(sem("bc_ready"), 1)
            dve.wait_ge(bank_free, FILL["ab_in"] + 8)

            def ssm_tile(j):
                dve.wait_ge(sem("bu_ready"), j + 1)
                bu = bank[j % 3][:].rearrange("p (a b) -> p a b", a=2)
                nc.vector.tensor_tensor(rot_a, bu, e_re[:, j, :].unsqueeze(1).broadcast_to([P, 2, T]), ALU.mult)
                nc.vector.tensor_tensor(rot_b, bu, e_im[:, j, :].unsqueeze(1).broadcast_to([P, 2, T]), ALU.mult).then_inc(sem("bu_used"), 1)
                dve.wait_ge(sem("bu_used"), j + 1)
                n0_ = chain.on(nc.vector.tensor_tensor(rot_w[:, 0, :], rot_a[:, 0, :], rot_b[:, 1, :], ALU.add))
                n1_ = chain.on(nc.vector.tensor_tensor(rot_w[:, 1, :], rot_a[:, 1, :], rot_b[:, 0, :], ALU.subtract))
                if j >= 2:
                    dve.wait_ge(sem("state_ready"), j - 1)
                for e, n in enumerate((n0_, n1_)):
                    chain_wait(n)
                    ins = nc.vector.tensor_tensor_scan(z_buf[j % 2][:, e, :], mag[:, j:j + 1].broadcast_to([P, T]), rot_w[:, e, :],
                                                       0.0, ALU.mult, ALU.add)
                ins.then_inc(sem("scan_done"), 1)
                if j % 4 == 3:
                    n = j // 4
                    if n >= 1:
                        y_out(n - 1)

            def y_out(n):
                c0 = COL["ssm_d"] + n
                dve.wait_ge(sem("ssm_y_done"), 4 * n + 4)
                nc.vector.scalar_tensor_tensor(y_ssm[:, n, :], u_t[:, n, :], par[:, c0:c0 + 1], bank[4 + n % 2][:, 0:T],
                                               ALU.mult, ALU.add).then_inc(sem("y_ready"), 1)

            def head(h):
                dve.wait_ge(sem("scores_done"), h + 1)
                if h % 4 == 0:
                    dve.wait_ge(sem(f"bias_back{h // 4}"), 128)
                s = hf[:, 2 * (h % 2):2 * (h % 2) + 2, :]
                k = 4 * (h % 2)
                if h >= 2:
                    dve.wait_ge(sem("probs_turned"), h - 1)
                nc.vector.scalar_tensor_tensor(s, bank[3][:].rearrange("p (a b) -> p a b", a=2), HD ** -0.5,
                                               sq[:, 2 * (h % 4):2 * (h % 4) + 2, :], ALU.mult, ALU.add).then_inc(sem("scores_used"), 1)
                dve.wait_ge(sem("scores_used"), h + 1)
                nc.vector.tensor_reduce(small[:, k:k + 2], s, AX_X, ALU.max, negate=True).then_inc(sem("peak_ready"), 1)
                dve.wait_ge(sem("exp_ready"), h + 1)
                link(nc.vector.reciprocal(small[:, k + 2:k + 4], small[:, k + 2:k + 4]))
                for qt in range(2):
                    ins = nc.vector.tensor_scalar(s[:, qt, :], s[:, qt, :], small[:, k + 2 + qt:k + 3 + qt], None, ALU.mult)
                ins.then_inc(sem("probs_ready"), 1)

            for h in range(HEADS):
                ssm_tile(2 * h)
                ssm_tile(2 * h + 1)
                head(h)
            y_out(UT - 1)
            dve.wait_ge(sem("part_hi"), 1)
            nc.vector.tensor_tensor(a_lo[:, 0:UT, :], y_ssm, a_hi[:, 0:UT, :].bitcast(F32), ALU.subtract).then_inc(sem("part_ready"), 1)
            lo_upto(Q["glu"] + 3)
            dve.wait_ge(bank_free, FILL["glu"] + 2)
            nc.vector.tensor_tensor(u_t, u_t, y_ssm, ALU.mult).then_inc(sem("ssm_out"), 1)
            dve.wait_ge(sem("part_hi"), 2)
            nc.vector.tensor_tensor(h_lo[:, 0:UT, :], u_t, h_hi[:, 0:UT, :].bitcast(F32), ALU.subtract)
            nc.vector.tensor_tensor(h_lo[:, UT:, :], q_t, h_hi[:, UT:, :].bitcast(F32), ALU.subtract).then_inc(sem("part_ready"), 1)

            def add_to_x(name, l, g):
                for c in range(4):
                    dve.wait_ge(chunk_done, Q[name] + c + 1)
                    for e in range(2):
                        k = 2 * c + e
                        ins = nc.vector.scalar_tensor_tensor(x[:, k, :], half(4 + (FILL[name] + c) % 2, e), mod[:, l, g + k:g + k + 1],
                                                             x[:, k, :], ALU.mult, ALU.add)
                    ins.then_inc(bank_free, 1)
                    lo_upto(Q[name] + c + 3)

            add_to_x("ab_out", 0, 16)
            gain(par[:, COL["norm_g"] + 8:COL["norm_g"] + 16], mod[:, 0, 32:40])
            norm(1, x[:], DT, lambda k: gains[:, 0, k:k + 1], lambda k: mod[:, 0, 24 + k:25 + k], h_hi[:], h_lo[:])

            def ffn(f, l, b0, c0):
                last, two = f == LAST_FFN, f >= 2
                q0, wb, wu, _, _ = ffn_columns(f)
                done = f * (FT // 2)

                def taps(dst, b, w, s):
                    n = [None, None]
                    shifts = ((0, 1), (2, -1)) if two else ((1, 1), (0, 2))
                    for k, (tap, d) in enumerate(shifts):
                        for e in range(2):
                            if k:
                                chain_wait(n[e])
                            o, src = (dst[:, e, d:], half(b, e)[:, 0:T - d]) if d > 0 else (dst[:, e, 0:T - 1], half(b, e)[:, 1:T])
                            ins = nc.vector.scalar_tensor_tensor(o, src, par[:, bass.ds(w[tap] + 2 * s + e, 1)], o, ALU.mult, ALU.add)
                            if not k:
                                n[e] = chain.on(ins)
                    return ins

                def step(s, q, i=None):
                    more_q = 0 if i is None else 6 * i
                    steps = done + s
                    dve.wait_ge(sem("tap_ready"), steps + 1)
                    taps(gate_c, 4, wb, s).then_inc(sem("conv_done"), 1)
                    yield
                    value = bank[5][:].rearrange("p (a b) -> p a b", a=2)
                    if two:
                        dve.wait_ge(sem("up_tap_ready"), (f - 2) * (FT // 2) + s + 1)
                        taps(up_c, 5, wu, s).then_inc(sem("up_done"), 1)
                        value = up_c
                        dve.wait_ge(sem("up_done"), (f - 2) * (FT // 2) + s + 1)
                    dve.wait_ge(sem("silu_ready"), steps + 1)
                    dve.wait_ge(chunk_done, q + 2 + more_q)
                    if steps_before(f, s):
                        dve.wait_ge(sem("act_hi"), steps)
                    nc.vector.tensor_tensor(act_f, value, gate_s, ALU.mult).then_inc(sem("act_ready"), 1)
                    yield
                    dve.wait_ge(sem("act_hi"), steps + 1)
                    k = 2 * (((q - q0 + 1) // 3) % 2)
                    nc.vector.tensor_tensor(a_lo[:, k:k + 2, :], act_f, a_hi[:, k:k + 2, :].bitcast(F32), ALU.subtract)\
                        .then_inc(sem("act_lo"), 1)
                    yield

                def run(s, q, nq, i, blocks):
                    g = step(s, q, i)
                    for k in range(3):
                        next(g)
                        if nq + k < NQ or i is not None:
                            lo(nq + k, i)
                        if b0 is not None and k in blocks:
                            mod_block(b0 + blocks[k], c0, i)

                g = step(0, q0)
                next(g)
                lo(q0 + 3)
                next(g)
                lo(q0 + 4)
                next(g)
                turns = 4 if last else 5
                start = chain.n
                per_turn = (8 if two else 4) + (3 * 6 if b0 is not None else 0)
                with dve.Fori(0, turns) as i:
                    more[0] = per_turn * i
                    run(2 * i + 1, q0 + 2, q0 + 5, i, {0: 0, 2: 1})
                    run(2 * i + 2, q0 + 5, q0 + 8, i, {1: 2})
                assert chain.n - start == per_turn, (chain.n - start, per_turn)
                chain.n = start + turns * per_turn
                more[0] = 0
                if last:
                    run(9, q0 + 26, q0 + 29, None, {})
                    run(10, q0 + 29, q0 + 32, None, {})
                nxt[0] = q0 + 35
                if b0 is not None:
                    mod_block(b0 + 15, c0)
                lo_upto(q0 + 35)
                dve.wait_ge(chunk_done, q0 + 33)
                for k in range(DT):
                    ins = nc.vector.scalar_tensor_tensor(x[:, k, :], half(k // 2, k % 2), mod[:, l, 40 + k:41 + k], x[:, k, :],
                                                         ALU.mult, ALU.add)
                ins.then_inc(sem("x_ready"), 1)
                if b0 is not None:
                    mod_out((1, 3)[f], b0 + MOD_BLOCKS, ("mod_b", "mod_b_2")[f], (48, 0)[f])

            ffn(0, 0, MB[1], 0)

            def layer(l):
                return [mod[:, l, 8 * i:8 * i + 8] for i in range(6)]

            def columns(name, k=0):
                return par[:, COL[name] + 8 * k:COL[name] + 8 * k + 8]

            def bias_to_x(name, l):
                link(nc.vector.tensor_tensor(g1b[:], mod[:, l, 16:24], columns(name), ALU.mult))
                for k in range(DT):
                    ins = nc.vector.tensor_scalar(x[:, k, :], x[:, k, :], g1b[:, k:k + 1], None, ALU.add)
                link(ins)

            def mixer_norm(n, l, g):
                gain(g, mod[:, l, 8:16])
                norm(n, x[:], DT, lambda k: gains[:, 0, k:k + 1], lambda k: mod[:, l, k:k + 1], h_hi[:], h_lo[:])

            def ffn_norm(n, l, g):
                gain(g, mod[:, l, 32:40])
                norm(n, x[:], DT, lambda k: gains[:, 0, k:k + 1], lambda k: mod[:, l, 24 + k:25 + k], h_hi[:], h_lo[:])

            def plain_norm(n, src, g):
                dve.wait_ge(sem("std_ready"), n + 1)
                nc.vector.reciprocal(rstd[:], std[:]).then_inc(sem("rstd_ready"), 1)
                dve.wait_ge(sem("rstd_ready"), n + 1)
                link(nc.vector.tensor_tensor(src, src, rstd[:].unsqueeze(1).broadcast_to([P, src.shape[1], T]), ALU.mult))
                for k in range(src.shape[1]):
                    ins = nc.vector.tensor_scalar(src[:, k, :], src[:, k, :], g(k), None, ALU.mult)
                return ins

            mixer_norm(2, 1, columns("norm_g", 2))
            nc.vector.memset(padded[:, :, 0:TAPS - 1], 0.0)
            for p in range(4):
                q, fill = Q["cm_in"] + 2 * p, FILL["cm_in"] + 2 * p
                lo_upto(q + 3)
                dve.wait_ge(sem("sig_ready"), p + 1)
                for e in range(2):
                    k = 2 * p + e
                    c0 = COL["cm_b_in"] + k
                    ins = nc.vector.scalar_tensor_tensor(padded[:, k, TAPS - 1:], half(4 + fill % 2, e), par[:, c0:c0 + 1], sig[:, e, :],
                                                         ALU.add, ALU.mult)
                ins.then_inc(bank_free, 2)
                lo_upto(q + 4)
            dve.wait_ge(bank_free, FILL["cm_in"] + 8)
            wt, bt = COL["cm_dw_w"], COL["cm_dw_b"]
            start = chain.n
            for k in range(DT):
                chain.on(nc.vector.tensor_scalar(hf[:, k, :], padded[:, k, 0:T], par[:, wt + k:wt + k + 1], par[:, bt + k:bt + k + 1],
                                                 ALU.mult, ALU.add))
            with dve.Fori(0, TAPS - 1) as i:
                more[0] = DT * i
                for k in range(DT):
                    chain_wait(start + k + 1)
                    ins = nc.vector.scalar_tensor_tensor(hf[:, k, :], padded[:, k, bass.ds(i + 1, T)], par[:, bass.ds(wt + DT * (i + 1) + k, 1)],
                                                         hf[:, k, :], ALU.mult, ALU.add)
                    chain.on(ins)
            more[0] = 0
            chain.n = start + DT * TAPS
            nc.vector.wait_ge(chain.sem, chain.n)
            nc.vector.tensor_copy(small[:, 31:32], eps[:]).then_inc(sem("conv_out"), 1)
            dve.wait_ge(sem("ctx_mod_done"), CTX_BLOCKS)
            link(nc.vector.tensor_tensor(mod[:, 2, 0:16], bank[3][:, 0:16], par[:, COL["mod_b_2"]:COL["mod_b_2"] + 16], ALU.add))
            dve.wait_ge(sem("mean_sum"), 1)
            link(nc.vector.tensor_scalar(mean, bank[6][:, 0:T], 1.0 / D, None, ALU.mult))
            nc.vector.tensor_tensor(hf[:], hf[:], mean.unsqueeze(1).broadcast_to([P, DT, T]), ALU.subtract).then_inc(sem("centered"), 1)
            dve.wait_ge(sem("std_ready"), 4)
            nc.vector.reciprocal(rstd[:], std[:]).then_inc(sem("rstd_ready"), 1)
            dve.wait_ge(sem("rstd_ready"), 4)
            nc.vector.tensor_tensor(hf[:], hf[:], rstd[:].unsqueeze(1).broadcast_to([P, DT, T]), ALU.mult).then_inc(sem("ln_ready"), 1)
            bias_to_x("cm_b_out", 1)
            dve.wait_ge(sem("ln_silu"), 1)
            link(nc.vector.tensor_copy(h_hi[:], hf[:]))
            nc.vector.tensor_tensor(h_lo[:], hf[:], h_hi[:].bitcast(F32), ALU.subtract).then_inc(sem("h_ready"), 1)
            add_to_x("cm_out", 1, 16)
            ffn_norm(4, 1, columns("norm_g", 3))
            ffn(1, 1, MB[3], 8)
            plain_norm(5, x[:], lambda k: par[:, COL["final_g"] + k:COL["final_g"] + k + 1]).then_inc(sem("x_ready"), 1)

            for b in range(4):
                dve.wait_ge(sem("ctx_turned"), b + 1)
                ins = nc.vector.tensor_copy(ctx_t[:, 2 * b:2 * b + 2, :], bank[b][:].rearrange("p (a b) -> p a b", a=2))
            ins.then_inc(sem("ctx_ready"), 1)
            mixer_norm(6, 3, columns("norm_mix_g_2"))
            gain(columns("norm_mix_g_2"), mod[:, 2, 8:16])
            norm(7, ctx_t, DT, lambda k: gains[:, 0, k:k + 1], lambda k: mod[:, 2, k:k + 1], a_hi[:], a_lo[:])
            for c in range(2):
                lo_upto(Q["dq"] + c + 3)
            lo_upto(Q["dkv"] + 3)
            dve.wait_ge(sem("k_turned"), 1)
            dve.wait_ge(sem("rope_landed"), 48)
            link(nc.vector.tensor_tensor(q_p[:, 0, :], bank[2][:, 0:T], rope_sin, ALU.mult))
            link(nc.vector.tensor_tensor(k_pe[:, 1, :], k_pe[:, 1, :], rope_cos, ALU.mult))
            nc.vector.tensor_tensor(k_pe[:, 1, :], k_pe[:, 1, :], q_p[:, 0, :], ALU.add).then_inc(sem("k_pe_ready"), 1)

            def split(n, src, g, hi_, lo_):
                link(plain_norm(n, src, g))
                link(nc.vector.tensor_copy(hi_, src))
                return nc.vector.tensor_tensor(lo_, src, hi_.bitcast(F32), ALU.subtract)

            split(8, c_q, lambda k: par[:, COL["mla_g_q_2"] + k:COL["mla_g_q_2"] + k + 1], h_hi[:, 0:QL // P, :], h_lo[:, 0:QL // P, :])\
                .then_inc(sem("h_ready"), 1)
            for e in range(2):
                split(9 + e, c_kv[:, :, e, :], lambda k: par[:, COL["mla_g_kv_2"] + k:COL["mla_g_kv_2"] + k + 1], kv_part(a_hi)[:, :, e, :],
                      kv_part(a_lo)[:, :, e, :]).then_inc(sem("h_ready"), 1)
            lo_upto(Q["dkv"] + 4)
            for c in range(3):
                lo_upto(Q["uq"] + c + 3)
            dve.wait_ge(bank_free, FILL["uq"] + 6)
            link(nc.vector.tensor_tensor(q_p, q_raw, rope_cos.unsqueeze(1).broadcast_to([P, 4, T]), ALU.mult))
            for b in range(2):
                dve.wait_ge(sem("q_turned"), b + 1)
                ins = nc.vector.tensor_tensor(q_raw[:, 2 * b:2 * b + 2, :], bank[b][:].rearrange("p (a b) -> p a b", a=2),
                                              rope_sin.unsqueeze(1).broadcast_to([P, 2, T]), ALU.mult)
            link(ins)
            nc.vector.tensor_tensor(q_p, q_p, q_raw, ALU.add).then_inc(sem("q_pe_ready"), 1)
            lo_upto(Q["ukv"] + 4)

            def mla_peak(h):
                for t in range(2):
                    u = 2 * h + t
                    k = 8 * (h % 2) + 4 * t
                    dve.wait_ge(sem("mla_scores"), u + 1)
                    link(nc.vector.tensor_reduce(small[:, k:k + 1], bank[u % 4][:], AX_X, ALU.max))
                    nc.vector.tensor_scalar(small[:, k + 1:k + 2], small[:, k:k + 1], -MLA_SCALE, None, ALU.mult).then_inc(sem("mla_peak"), 1)

            mla_peak(0)
            for h in range(MH):
                if h + 1 < MH:
                    mla_peak(h + 1)
                for t in range(2):
                    k = 8 * (h % 2) + 4 * t
                    dve.wait_ge(sem("mla_exp"), 2 * h + t + 1)
                    link(nc.vector.reciprocal(small[:, k + 3:k + 4], small[:, k + 2:k + 3]))
                    ins = nc.vector.tensor_scalar(mla_s(h, t), mla_s(h, t), small[:, k + 3:k + 4], None, ALU.mult)
                ins.then_inc(sem("mla_probs"), 1)
                dve.wait_ge(sem("mla_turned"), h + 1)
                if h >= 2:
                    dve.wait_ge(sem("mla_head"), h - 1)
                nc.vector.tensor_copy(mla_p(h)[:, 2:4, :], bank[5][:].rearrange("p (a b) -> p a b", a=2)).then_inc(sem("mla_pt1"), 1)
                mod_block(MB[4] + h, 8)
            mod_out(4, MB[4] + MOD_BLOCKS, "mod_b_2", 48)
            dve.wait_ge(sem("part_hi"), 3)
            nc.vector.tensor_tensor(h_lo[:], q_n, h_hi[:].bitcast(F32), ALU.subtract).then_inc(sem("part_ready"), 1)
            add_to_x("mla_out", 3, 16)
            ffn_norm(11, 3, columns("norm_ffn_g_2"))
            ffn(2, 3, None, None)

            mixer_norm(12, 4, columns("norm_mix_g_2", 1))
            cw, cb = COL["hy_conv_w_2"], COL["hy_conv_b_2"]
            for c in range(12):
                q, fill = Q["hy_in"] + c, FILL["hy_in"] + c
                lo_upto(q + 3)
                dve.wait_ge(bank_free, fill + 1)
                zb = z_b[c % 2]
                n = [0, 0]
                for tap, d in ((1, 0), (0, 1), (2, -1)):
                    for e in range(2):
                        k = 2 * c + e
                        w = par[:, cw + 24 * tap + k:cw + 24 * tap + k + 1]
                        if tap == 1:
                            ins = nc.vector.tensor_scalar(z_c[:, k, :], zb[:, e, :], w, par[:, cb + k:cb + k + 1], ALU.mult, ALU.add)
                        else:
                            chain_wait(n[e])
                            o, i_ = (z_c[:, k, 1:], zb[:, e, 0:T - 1]) if d > 0 else (z_c[:, k, 0:T - 1], zb[:, e, 1:])
                            ins = nc.vector.scalar_tensor_tensor(o, i_, w, o, ALU.mult, ALU.add)
                        if tap != 2:
                            n[e] = chain.on(ins)
                ins.then_inc(sem("hy_conv"), 1)
                if c >= 8:
                    dve.wait_ge(sem("hy_conv"), c + 1)
                    k = 2 * c
                    nc.vector.tensor_tensor(z_c[:, k:k + 2, :], z_c[:, k:k + 2, :], z_c[:, k - DT:k - DT + 2, :], ALU.mult).then_inc(sem("v_ready"), 1)
                if c < 2:
                    dve.wait_ge(sem("hy_mlp"), c + 1)
                    if c:
                        dve.wait_ge(sem("hy_hid"), 1)
                    else:
                        dve.wait_ge(sem("hy_landed"), 16 * 11)
                    link(nc.vector.tensor_scalar(angle[1], bank[c][0:HY_HID, 0:T], hy_cols[0:HY_HID, 2 * c:2 * c + 1],
                                                 hy_cols[0:HY_HID, 2 * c + 1:2 * c + 2], ALU.add, ALU.mult))
                    reduce_angle(angle[0], angle[1], hy_tmp).then_inc(sem("hy_angle"), 1)
                elif c < 4:
                    t = c - 2
                    dve.wait_ge(sem("hy_window"), t + 1)
                    dve.wait_ge(sem("hy_taps"), t + 1)
                    for b in range(2):
                        part = slice(512 * b, 512 * b + 512)
                        nc.vector.tensor_tensor(hy_fwd[:, part], bank[b][:], hy_window[:, t, part], ALU.mult)
                        ins = nc.vector.tensor_tensor(hy_bwd[:, part], bank[2 + b][:], hy_window[:, t, part], ALU.mult)
                    link(ins)
                    if t == 0:
                        link(nc.vector.memset(hy_bwd[0:1, :], 0.0))
                    nc.vector.tensor_tensor(hy_s[:, t, :], hy_fwd, hy_bwd, ALU.add)
                    nc.vector.tensor_tensor(hy_d[:, t, :], hy_fwd, hy_bwd, ALU.subtract).then_inc(sem("filter_taps"), 1)
            for s_ in range(2):
                dve.wait_ge(sem("spectrum"), s_ + 1)
                dve.wait_ge(sem("filter_ready"), 2)
                part = slice(512 * s_, 512 * s_ + 512)
                for ft in range(2):
                    fr, fi = f_re[:, ft, part], f_im[:, ft, part]
                    ur, ui = bank[ft][:], bank[2 + ft][:]
                    p0, p1, p2, p3 = (hf[:, 2 * i:2 * i + 2, :].rearrange("p a b -> p (a b)") for i in range(4))
                    nc.vector.tensor_tensor(p0, ur, fr, ALU.mult)
                    n0_ = chain.on(nc.vector.tensor_tensor(p1, ui, fi, ALU.mult))
                    nc.vector.tensor_tensor(p2, ur, fi, ALU.mult)
                    n1_ = nc.vector.tensor_tensor(p3, ui, fr, ALU.mult)
                    n1_ = chain.on(n1_)
                    chain_wait(n0_)
                    link(nc.vector.tensor_tensor(y_re[:, ft, part], p0, p1, ALU.subtract))
                    chain_wait(n1_)
                    ins = nc.vector.tensor_tensor(y_im[:, ft, part], p2, p3, ALU.add)
                    if ft == 0:
                        link(ins)
                ins.then_inc(sem("product"), 1)
                dve.wait_ge(sem("product"), s_ + 1)
            bias_to_x("hy_b_out_2", 4)
            for c in range(4):
                fill = FILL["hy_y"] + c
                dve.wait_ge(sem("hy_y_done"), c + 1)
                for e in range(2):
                    k = 2 * c + e
                    c0 = COL["hy_d_bias_2"] + k
                    ins = nc.vector.scalar_tensor_tensor(z_c[:, DT + k, :], z_c[:, 2 * DT + k, :], par[:, c0:c0 + 1],
                                                         half(4 + fill % 2, e), ALU.mult, ALU.add)
                ins.then_inc(bank_free, 1)
                dve.wait_ge(bank_free, fill + 1)
                k = 2 * c
                nc.vector.tensor_tensor(z_c[:, DT + k:DT + k + 2, :], z_c[:, DT + k:DT + k + 2, :], z_c[:, k:k + 2, :], ALU.mult)\
                    .then_inc(sem("hy_y_ready"), 1)
            dve.wait_ge(sem("part_hi"), 4)
            nc.vector.tensor_tensor(h_lo[:], z_c[:, DT:2 * DT, :], h_hi[:].bitcast(F32), ALU.subtract).then_inc(sem("part_ready"), 1)
            add_to_x("hy_out", 4, 16)
            ffn_norm(13, 4, columns("norm_ffn_g_2", 1))
            ffn(3, 4, None, None)
            plain_norm(14, x[:], lambda k: par[:, COL["final_g_2"] + k:COL["final_g_2"] + k + 1]).then_inc(sem("x_ready"), 1)
            for t in range(2):
                dve.wait_ge(sem("x_back"), t + 1)
                for b in range(2):
                    ins = nc.vector.tensor_copy(out_tok[:, t, 512 * b:512 * b + 512], bank[2 * t + b][:])
                ins.then_inc(sem("out_turned"), 1)

        @block.tensor
        def _(pe):
            def turn(out_, in_, n=P):
                return nc.tensor.transpose(out_, in_, ident[0:n, 0:n])

            def mod_turn(b, column, i=None):
                ring = mla_mod_acc if b >= MB[4] else mod_acc
                pe.wait_ge(sem("mod_used"), 2 * b + 2 + (0 if i is None else 6 * i))
                for n in range(3):
                    for e in range(2):
                        ins = nc.tensor.matmul(bank[6][:, bass.ds(column + n, 1)], ring[b % len(ring)][:, e, n * P:(n + 1) * P], ones[:, 0:1],
                                               start=(e == 0), stop=(e == 1))
                ins.then_inc(sem("mod_turned"), 1)

            pe.wait_ge(sem("ident_landed"), 16)
            pe.wait_ge(sem("c_landed"), 48)
            turn(bank[7][:, 0:24], c_rows, 24).then_inc(sem("c_turned"), 1)
            pe.wait_ge(sem("const_ready"), 1)
            for b in range(4):
                mod_turn(b, 3 * b)
            pe.wait_ge(sem("par_landed"), 16 * len(par_pieces))
            for t in range(PAR_T):
                n = min(P, PAR_ROWS - P * t)
                ins = turn(bank[t // 4][:, (t % 4) * P:(t % 4) * P + n], par_raw[0:n, t, :], n)
                if t % 4 == 3 or t == PAR_T - 1:
                    ins.then_inc(sem("par_turned"), 1)
            pe.wait_ge(sem("x_landed"), 16)
            pe.wait_ge(sem("par_ready"), 3)
            for k in range(DT):
                for t in range(2):
                    ins = turn(bank[k // 2][:, (k % 2) * T + t * P:(k % 2) * T + (t + 1) * P], xtok[:, t, k * P:(k + 1) * P])
                if k % 2:
                    ins.then_inc(sem("x_turned"), 1)
            pe.wait_ge(sem("tab_landed"), 48)
            nc.tensor.matmul(bank[7][0:HEADS, :], tab[:], hot, start=True, stop=True).then_inc(sem("bias_row_done"), 1)

            for b in range(4, MOD_BLOCKS):
                mod_turn(b, 3 * b)

            def norm_sum(n, kt=DT, src=None):
                pe.wait_ge(sem("sq_ready"), n + 1)
                for k in range(kt):
                    ins = nc.tensor.matmul(bank[7][:, 0:T], ones[:], sq[:, k, :], start=(k == 0), stop=(k == kt - 1))
                ins.then_inc(sem("norm_sum"), 1)

            def three(out_, w_parts, h_parts, first, last, swap=False, **kw):
                pairs = ((0, 0), (0, 1), (1, 0))
                for n, (a, b) in enumerate(pairs):
                    l, r = (h_parts[b], w_parts[a]) if swap else (w_parts[a], h_parts[b])
                    ins = nc.tensor.matmul(out_, l, r, start=first and n == 0, stop=last and n == 2, **kw)
                return ins

            def chunk_ready(q, i=None):
                pe.wait_ge(lo_done, q + 1 + (0 if i is None else 6 * i))

            def w_at(q, k, kt, c0, n=P):
                s, w = q % SLOTS, CHUNK // kt
                return w_hi[s][:, k * w + c0:k * w + c0 + n], w_lo[s][:, k * w + c0:k * w + c0 + n]

            def feature_chunk(q, fill, kt, hh, hl, i=None, finish=True, b=None):
                chunk_ready(q, i)
                tiles = CHUNK // kt // P
                for n in range(tiles):
                    if fill is not None and n % 2 == 0 and fill + n // 2 >= 2:
                        pe.wait_ge(bank_free, fill + n // 2 - 1 + (0 if i is None else 4 * i))
                    bb = 4 + (fill + n // 2) % 2
                    for k in range(kt):
                        ins = three(half(bb, n % 2), w_at(q, k, kt, n * P), (hh[:, k, :], hl[:, k, :]), k == 0, k == kt - 1)
                ins.then_inc(chunk_done, 1)

            norm_sum(0)
            pe.wait_ge(sem("h_ready"), 1)
            for c in range(6):
                feature_chunk(Q["ab_in"] + c, FILL["ab_in"] + c, DT, h_hi, h_lo)
                if c == 0:
                    pe.wait_ge(sem("bc_wide"), 1)
                    for e in range(2):
                        for t in range(UT):
                            ins = turn(bank[e][:, t * P:(t + 1) * P], b_wide[:, e, 4 * t:4 * t + 4, :].rearrange("p a b -> p (a b)"))
                        ins.then_inc(sem("bc_turned"), 1)
                    for e in range(2):
                        for t in range(UT):
                            ins = turn(bank[2 + e][:, t * P:(t + 1) * P], c_wide[:, e, t, :])
                        ins.then_inc(sem("bc_turned"), 1)
            for c in range(6, 8):
                q, fill = Q["ab_in"] + c, FILL["ab_in"] + c
                chunk_ready(q)
                pe.wait_ge(bank_free, fill - 1)
                for t in range(2):
                    for k in range(DT):
                        tok = slice(t * P, (t + 1) * P)
                        ins = three(half(4 + fill % 2, t), w_at(q, k, DT, 0, 256), (h_hi[:, k, tok], h_lo[:, k, tok]),
                                    k == 0, k == DT - 1, swap=True)
                ins.then_inc(chunk_done, 1)

            def bu(j):
                if j >= 3:
                    pe.wait_ge(sem("bu_used"), j - 2)
                r = slice(32 * (j % 4), 32 * (j % 4) + 32)
                for e in range(2):
                    ins = nc.tensor.matmul(half(j % 3, e), b_turned[r, e, j // 4, :], u_t[r, j // 4, :], start=True, stop=True)
                ins.then_inc(sem("bu_ready"), 1)

            def y_of(j):
                pe.wait_ge(sem("state_ready"), j + 1)
                r = 32 * (j % 4)
                if j >= 8 and j % 4 == 0:
                    pe.wait_ge(sem("y_ready"), j // 4 - 1)
                for e in range(2):
                    ins = nc.tensor.matmul(bank[4 + j // 4 % 2][r:r + 32, 0:T], c_turned[:, e, j // 4, r:r + 32], s_buf[j % 2][:, e, :],
                                           start=(e == 0), stop=(e == 1))
                ins.then_inc(sem("ssm_y_done"), 1)

            def scores(h):
                if h >= 1:
                    pe.wait_ge(sem("scores_used"), h)
                r = slice(64 * (h % 2), 64 * (h % 2) + 64)
                for t in range(2):
                    ins = nc.tensor.matmul(half(3, t), q_t[r, h // 2, t * P:(t + 1) * P], k_t[r, h // 2, :], start=True, stop=True)
                ins.then_inc(sem("scores_done"), 1)

            def head_out(h):
                pe.wait_ge(sem("probs_ready"), h + 1)
                if h >= 1:
                    pe.wait_ge(sem("probs_t"), h)
                for kt in range(2):
                    for qt in range(2):
                        ins = turn(bank[6][:, kt * T + qt * P:kt * T + (qt + 1) * P], hf[:, 2 * (h % 2) + qt, kt * P:(kt + 1) * P])
                ins.then_inc(sem("probs_turned"), 1)
                pe.wait_ge(sem("probs_t"), h + 1)
                if h >= 1:
                    pe.wait_ge(sem("att_out"), h)
                r = 64 * (h % 2)
                for kt in range(2):
                    ins = nc.tensor.matmul(bank[7][r:r + 64, 0:T], v_tok[:, kt, h * HD:(h + 1) * HD], hf[:, 4 + 2 * (h % 2) + kt, :],
                                           start=(kt == 0), stop=(kt == 1))
                ins.then_inc(sem("head_done"), 1)

            pe.wait_ge(bank_free, FILL["ab_in"] + 8)
            pe.wait_ge(sem("bc_ready"), 1)
            bu(0)
            bu(1)
            scores(0)
            for h in range(HEADS):
                if h + 1 < HEADS:
                    bu(2 * h + 2)
                    bu(2 * h + 3)
                    scores(h + 1)
                y_of(2 * h)
                y_of(2 * h + 1)
                head_out(h)
            pe.wait_ge(sem("part_ready"), 1)
            feature_chunk(Q["glu"], FILL["glu"], UT, a_hi, a_lo)
            pe.wait_ge(sem("part_ready"), 2)
            for c in range(4):
                feature_chunk(Q["ab_out"] + c, FILL["ab_out"] + c, DT, h_hi, h_lo)
            norm_sum(1)

            def ffn(f, b0):
                q0 = Q[f"ffn{f}"]
                done = f * (FT // 2)
                pe.wait_ge(sem("h_ready"), FFN_INPUT[f])
                for b in range(4):
                    nc.tensor.matmul(bank[b][:], zeros[:, 0:P], zeros[:], start=True, stop=False, skip_group_check=True)

                def up_gate(s, q, i=None):
                    more = 0 if i is None else 6 * i
                    for j in range(2):
                        chunk_ready(q + j, i)
                        if j == 0:
                            pe.wait_ge(sem("conv_done"), done + s) if steps_before(f, s) else None
                        else:
                            pe.wait_ge(sem("act_ready"), done + s) if steps_before(f, s) else None
                        for n in range(2):
                            for k in range(DT):
                                ins = three(half(4 + j, n), w_at(q + j, k, DT, n * P), (h_hi[:, k, :], h_lo[:, k, :]), k == 0, k == DT - 1)
                        ins.then_inc(chunk_done, 1)

                def down(s, q, i=None, last=False):
                    chunk_ready(q, i)
                    pe.wait_ge(sem("act_lo"), done + s + 1)
                    k0 = 0 if last else 2 * (((q - q0 - 4) // 3) % 2)
                    for k in range(2):
                        for n in range(DT):
                            ins = three(half(n // 2, n % 2), w_at(q, k, 2, n * P), (a_hi[:, k0 + k, :], a_lo[:, k0 + k, :]),
                                        False, last and k == 1, skip_group_check=True)
                    ins.then_inc(chunk_done, 1)

                up_gate(0, q0)
                with pe.Fori(0, 5) as i:
                    for e in range(2):
                        s, q = 2 * i + 1 + e, q0 + 2 + 3 * e
                        up_gate(s, q, i)
                        if b0 is not None and e:
                            mod_turn(b0 + 1, 9 * i + 3, i)
                        down(s - 1, q + 2, i)
                        if b0 is not None:
                            mod_turn(b0 + 2 * e, 9 * i + 6 * e, i)
                down(10, q0 + 32, last=True)
                if b0 is not None:
                    mod_turn(b0 + 15, 45)

            ffn(0, MB[1])

            def spectrum(sources, s_):
                for part in range(2):
                    for ft in range(2):
                        for t in range(2):
                            ins = nc.tensor.matmul(bank[2 * part + ft][:], dft[:, part, t, ft * P:(ft + 1) * P],
                                                   sources[part][:, t, 512 * s_:512 * s_ + 512], start=(t == 0), stop=(t == 1))
                return ins

            norm_sum(2)
            pe.wait_ge(sem("h_ready"), 3)
            for c in range(8):
                feature_chunk(Q["cm_in"] + c, FILL["cm_in"] + c, DT, h_hi, h_lo)
            for b in range(CTX_BLOCKS):
                pe.wait_ge(sem(f"ctx_mod_landed{b % 3}"), 16 * (b // 3 + 1))
                for n in range(CTX_COLS // P):
                    for k in range(DT):
                        col = b * (CTX_COLS // P) + n
                        ins = nc.tensor.matmul(bank[3][:, col:col + 1], ctx_w[b % 3][:, k, n * P:(n + 1) * P],
                                               silu_c[:, 16 + k:17 + k], start=(k == 0), stop=(k == DT - 1))
                ins.then_inc(sem("ctx_mod_done"), 1)
            pe.wait_ge(sem("conv_out"), 1)
            for k in range(DT):
                ins = nc.tensor.matmul(bank[6][:, 0:T], ones[:], hf[:, k, :], start=(k == 0), stop=(k == DT - 1))
            ins.then_inc(sem("mean_sum"), 1)
            norm_sum(3)
            pe.wait_ge(sem("h_ready"), 4)
            for c in range(4):
                feature_chunk(Q["cm_out"] + c, FILL["cm_out"] + c, DT, h_hi, h_lo)
            norm_sum(4)
            ffn(1, MB[3])
            norm_sum(5)

            pe.wait_ge(sem("ctx_landed"), 16)
            for k in range(DT):
                for t in range(2):
                    ins = turn(bank[k // 2][:, (k % 2) * T + t * P:(k % 2) * T + (t + 1) * P], ctx_tok[:, t, k * P:(k + 1) * P])
                if k % 2:
                    ins.then_inc(sem("ctx_turned"), 1)
            norm_sum(6)
            norm_sum(7)
            pe.wait_ge(sem("h_ready"), 6)
            for c in range(2):
                feature_chunk(Q["dq"] + c, FILL["dq"] + c, DT, h_hi, h_lo)
            pe.wait_ge(sem("h_ready"), 7)
            for c in range(2):
                q = Q["dkv"] + c
                chunk_ready(q)
                for n in range(2 - c):
                    fill = FILL["dkv"] + 2 * c + n
                    pe.wait_ge(bank_free, fill - 1)
                    for e, (hh, hl) in enumerate(((a_hi, a_lo), (h_hi, h_lo))):
                        for k in range(DT):
                            ins = three(half(4 + fill % 2, e), w_at(q, k, DT, n * P), (hh[:, k, :], hl[:, k, :]), k == 0, k == DT - 1)
                ins.then_inc(chunk_done, 1)
            pe.wait_ge(bank_free, FILL["dkv"] + 3)
            pe.wait_ge(sem("rope_landed"), 48)
            nc.tensor.matmul(bank[2][:, 0:T], turn_w, k_pe[:, 1, :], start=True, stop=True).then_inc(sem("k_turned"), 1)
            norm_sum(8, QL // P)
            for e in range(2):
                norm_sum(9 + e, KVL // P)
            pe.wait_ge(sem("h_ready"), 8)
            for c in range(3):
                feature_chunk(Q["uq"] + c, FILL["uq"] + 2 * c, QL // P, h_hi, h_lo)
            pe.wait_ge(bank_free, FILL["uq"] + 6)
            for b in range(2):
                for e in range(2):
                    ins = nc.tensor.matmul(half(b, e), turn_w, q_raw[:, 2 * b + e, :], start=True, stop=True)
                ins.then_inc(sem("q_turned"), 1)
            pe.wait_ge(sem("h_ready"), 10)
            for c in range(2):
                q = Q["ukv"] + c
                chunk_ready(q)
                for n in range(8):
                    fill = FILL["ukv"] + 8 * c + n
                    pe.wait_ge(bank_free, fill - 1)
                    for k in range(KVL // P):
                        hh, hl = (kv_part(v)[:, k].rearrange("p a b -> p (a b)") for v in (a_hi, a_lo))
                        if c == 0:
                            ins = three(bank[4 + fill % 2][:], w_at(q, k, KVL // P, n * P), (hh, hl), k == 0, k == 1)
                        else:
                            tok = slice((n // 2) * P, (n // 2 + 1) * P)
                            ins = three(bank[4 + fill % 2][:], w_at(q, k, KVL // P, (n % 2) * 512, 512), (hh[:, tok], hl[:, tok]),
                                        k == 0, k == 1, swap=True)
                    ins.then_inc(chunk_done if n == 7 else sem("kv_filled"), 1)

            def mla_scores(h):
                for t in range(2):
                    u = 2 * h + t
                    if h >= 2:
                        pe.wait_ge(sem("mla_exp"), u - 3)
                    r, r2 = 64 * (h % 2), 32 * (h % 4)
                    nc.tensor.matmul(bank[u % 4][:], q_n[r:r + 64, h // 2, t * P:(t + 1) * P], k_n[r:r + 64, h // 2, :], start=True, stop=False)
                    nc.tensor.matmul(bank[u % 4][:], q_p[r2:r2 + 32, h // 4, t * P:(t + 1) * P],
                                     k_pe[r2:r2 + 32].rearrange("p a b -> p (a b)"), start=False, stop=True).then_inc(sem("mla_scores"), 1)

            pe.wait_ge(bank_free, FILL["ukv"] + 16)
            pe.wait_ge(sem("k_pe_ready"), 1)
            pe.wait_ge(sem("q_pe_ready"), 1)
            mla_scores(0)
            for h in range(MH):
                if h + 1 < MH:
                    mla_scores(h + 1)
                pe.wait_ge(sem("mla_probs"), h + 1)
                if h >= 1:
                    pe.wait_ge(sem("mla_pt0"), h)
                    pe.wait_ge(sem("mla_pt1"), h)
                for kt in range(4):
                    for t in range(2):
                        ins = turn(bank[4 + kt // 2][:, (kt % 2) * T + t * P:(kt % 2) * T + (t + 1) * P], mla_s(h, t)[:, kt * P:(kt + 1) * P])
                ins.then_inc(sem("mla_turned"), 1)
                pe.wait_ge(sem("mla_pt0"), h + 1)
                pe.wait_ge(sem("mla_pt1"), h + 1)
                if h >= 1:
                    pe.wait_ge(sem("mla_out"), h)
                r = 64 * (h % 2)
                for kt in range(4):
                    ins = nc.tensor.matmul(bank[7][r:r + 64, 0:T], v_mla[:, kt, h * VH:(h + 1) * VH], mla_p(h)[:, kt, :],
                                           start=(kt == 0), stop=(kt == 3))
                ins.then_inc(sem("mla_head"), 1)
                mod_turn(MB[4] + h, 3 * h)
            pe.wait_ge(sem("part_ready"), 3)
            for c in range(4):
                feature_chunk(Q["mla_out"] + c, FILL["mla_out"] + c, DT, h_hi, h_lo)
            norm_sum(11)
            ffn(2, None)

            norm_sum(12)
            pe.wait_ge(sem("h_ready"), 12)
            for c in range(12):
                feature_chunk(Q["hy_in"] + c, FILL["hy_in"] + c, DT, h_hi, h_lo)
                if c == 0:
                    pe.wait_ge(sem("hy_landed"), 16 * 11)
                if c < 2:
                    if c:
                        pe.wait_ge(sem("hy_hid"), 1)
                    nc.tensor.matmul(bank[c][0:HY_HID, 0:T], hy_w[c], (pos, hid[0])[c], start=True, stop=True).then_inc(sem("hy_mlp"), 1)
                elif c < 4:
                    t = c - 2
                    pe.wait_ge(sem("hy_hid"), 2)
                    pe.wait_ge(sem("hy_w3_landed"), 16)
                    if t:
                        pe.wait_ge(sem("filter_taps"), 1)
                    w3 = sq[0:HY_HID].rearrange("p a b -> p (a b)")
                    for b in range(4):
                        ins = nc.tensor.matmul(bank[b][:], hid[1][:, t * P:(t + 1) * P], w3[:, 512 * b:512 * b + 512], start=True, stop=True)
                    ins.then_inc(sem("hy_taps"), 1)
                elif c < 6:
                    pe.wait_ge(sem("filter_taps"), 2)
                    if c == 5:
                        pe.wait_ge(sem("filter_ready"), 1)
                    spectrum((hy_s, hy_d), c - 4).then_inc(sem("filter_done"), 1)
            for c in range(4):
                pe.wait_ge(sem("v_ready"), c + 1)
                if c >= 2:
                    pe.wait_ge(sem("hy_v_ready"), c - 1)
                for t in range(2):
                    for e in range(2):
                        ins = turn(bank[6 + c % 2][:, t * T + e * P:t * T + (e + 1) * P], z_c[:, 2 * DT + 2 * c + e, t * P:(t + 1) * P])
                ins.then_inc(sem("v_turned"), 1)
            pe.wait_ge(sem("filter_ready"), 2)
            for s_ in range(2):
                pe.wait_ge(sem("hy_v_ready"), 2 * s_ + 2)
                if s_:
                    pe.wait_ge(sem("product"), 1)
                spectrum((hy_v, hy_v), s_).then_inc(sem("spectrum"), 1)
            for c in range(4):
                fill = FILL["hy_y"] + c
                pe.wait_ge(sem("product"), c // 2 + 1)
                pe.wait_ge(bank_free, fill - 1)
                for e in range(2):
                    k = 2 * c + e
                    for part, y in enumerate((y_re, y_im)):
                        for ft in range(2):
                            ins = nc.tensor.matmul(half(4 + fill % 2, e), y[:, ft, k * P:(k + 1) * P], idft[:, part, ft, :],
                                                   start=(part + ft == 0), stop=(part + ft == 2))
                ins.then_inc(sem("hy_y_done"), 1)
            pe.wait_ge(sem("part_ready"), 4)
            for c in range(4):
                feature_chunk(Q["hy_out"] + c, FILL["hy_out"] + c, DT, h_hi, h_lo)
            norm_sum(13)
            ffn(3, None)
            norm_sum(14)
            pe.wait_ge(sem("x_ready"), 7)
            for t in range(2):
                for k in range(DT):
                    ins = turn(bank[2 * t + k // 4][:, (k % 4) * P:(k % 4 + 1) * P], x[:, k, t * P:(t + 1) * P])
                ins.then_inc(sem("x_back"), 1)


def kernel(**inputs):
    import concourse.bacc as bacc
    from concourse.bass_utils import run_bass_kernel_spmd

    nc = bacc.Bacc("TRN2", target_bir_lowering=False, num_devices=1, dynamic_dma_scratch_size=1024)
    arrays, A = {}, {}
    tables = consts()
    tables["masked"] = np.full((1, HEADS), MASKED, np.float32)
    up_2 = np.asarray(inputs.pop("ffn_w_up_2"))
    inputs["ffn_w_up_value_2"], inputs["ffn_w_up_gate_2"] = up_2[:, :, :F], up_2[:, :, F:]
    for name, a in list(inputs.items()) + list(tables.items()):
        a = np.ascontiguousarray(a)
        arrays["in_" + name] = a
        A[name] = nc.dram_tensor("in_" + name, a.shape, mybir.dt.from_np(a.dtype), kind="ExternalInput").ap()
    A["bias_row"] = nc.dram_tensor("bias_row", (HEADS, 2 * T), F32, kind="Internal").ap()
    A["bias_copies"] = nc.dram_tensor("bias_copies", (HEADS, P, 2 * T), F32, kind="Internal").ap()
    out = nc.dram_tensor("out", (T, D), F32, kind="ExternalOutput").ap()
    build(nc, A, out)
    r = run_bass_kernel_spmd(nc, [arrays], core_ids=[0])
    return r.results[0]["out"].reshape(1, T, D)
```
